# Optimizing a Trainium2 kernel written in Bass

```python
import math
import jax, jax.numpy as jnp
from jax import lax
import numpy as np

D_MODEL = 1024
BATCH = 1
SEQ = 512
DEPTH = 2

MLA_HEADS = 4
MLA_NOPE_DIM = 128
MLA_ROPE_DIM = 64
MLA_V_DIM = 128
MLA_Q_RANK = 256
MLA_KV_RANK = 128
DIFF_HEADS = 4
DIFF_HEAD_DIM = 64
MIX_WIDTH = MLA_HEADS * MLA_V_DIM + DIFF_HEADS * 2 * DIFF_HEAD_DIM
IN_SPLITS = (MLA_Q_RANK, MLA_KV_RANK, MLA_ROPE_DIM,
             DIFF_HEADS * 2 * DIFF_HEAD_DIM,
             DIFF_HEADS * 2 * DIFF_HEAD_DIM,
             DIFF_HEADS * 2 * DIFF_HEAD_DIM)
IN_WIDTH = sum(IN_SPLITS)
D_FF = 2816
Q_BLOCK = 128
ROPE_THETA = 10000.0
NORM_EPS = 1e-5
DEEPNORM_ALPHA = (2 * DEPTH) ** 0.25
DEEPNORM_BETA = (8 * DEPTH) ** -0.25

kernel_name = "hymba_mla_diffattn_macaron_deepnorm"

def layer_norm(x, g, b):
    xf = x.astype(jnp.float32)
    mu = jnp.mean(xf, axis=-1, keepdims=True)
    var = jnp.mean(jnp.square(xf - mu), axis=-1, keepdims=True)
    y = (xf - mu) * lax.rsqrt(var + NORM_EPS)
    return (y * g.astype(jnp.float32) + b.astype(jnp.float32)).astype(x.dtype)

def rms_norm(x, g):
    xf = x.astype(jnp.float32)
    y = xf * lax.rsqrt(jnp.mean(jnp.square(xf), axis=-1, keepdims=True) + NORM_EPS)
    return (y * g.astype(jnp.float32)).astype(x.dtype)

def swiglu(x, w_gate, w_up, w_down):
    return (jax.nn.silu(x @ w_gate) * (x @ w_up)) @ w_down

def rope_tables(pos, dim):
    inv_freq = ROPE_THETA ** (-jnp.arange(0, dim, 2, dtype=jnp.float32) / dim)
    ang = pos.astype(jnp.float32)[:, None] * inv_freq[None, :]
    return jnp.cos(ang), jnp.sin(ang)

def apply_rope(x, cos, sin):
    x1, x2 = jnp.split(x, 2, axis=-1)
    cos = cos.astype(x.dtype)
    sin = sin.astype(x.dtype)
    return jnp.concatenate([x1 * cos - x2 * sin, x2 * cos + x1 * sin], axis=-1)

def sweep_query_blocks(block_fn, *q_side):
    b, s = q_side[0].shape[:2]
    nb = s // Q_BLOCK
    blocks = tuple(jnp.swapaxes(a.reshape((b, nb, Q_BLOCK) + a.shape[2:]), 0, 1) for a in q_side)
    out = lax.map(lambda blk: block_fn(*blk), blocks)
    out = jnp.swapaxes(out, 0, 1)
    return out.reshape((b, s) + out.shape[3:])

def mla_mixer(c_q, c_kv, k_rope_raw, pos, q_norm_g, w_q_up, kv_norm_g, w_kv_up):
    b, s, _ = c_q.shape
    q = (rms_norm(c_q, q_norm_g) @ w_q_up).reshape(b, s, MLA_HEADS, MLA_NOPE_DIM + MLA_ROPE_DIM)
    q_nope, q_rope = q[..., :MLA_NOPE_DIM], q[..., MLA_NOPE_DIM:]
    kv = (rms_norm(c_kv, kv_norm_g) @ w_kv_up).reshape(b, s, MLA_HEADS, MLA_NOPE_DIM + MLA_V_DIM)
    k_nope, v = kv[..., :MLA_NOPE_DIM], kv[..., MLA_NOPE_DIM:]
    cos, sin = rope_tables(pos, MLA_ROPE_DIM)
    q_rope = apply_rope(q_rope, cos[:, None, :], sin[:, None, :])
    k_rope = apply_rope(k_rope_raw, cos, sin)
    q = jnp.concatenate([q_nope, q_rope], axis=-1)
    k = jnp.concatenate([k_nope, jnp.broadcast_to(k_rope[:, :, None, :], (b, s, MLA_HEADS, MLA_ROPE_DIM))], axis=-1)
    scale = (MLA_NOPE_DIM + MLA_ROPE_DIM) ** -0.5

    def block(qb):
        sc = jnp.einsum('bqhd,bkhd->bhqk', qb, k).astype(jnp.float32) * scale
        p = jax.nn.softmax(sc, axis=-1).astype(v.dtype)
        return jnp.einsum('bhqk,bkhd->bqhd', p, v)

    o = sweep_query_blocks(block, q)
    return o.reshape(b, s, MLA_HEADS * MLA_V_DIM)

def diff_mixer(q, k, v, pos, lq1, lk1, lq2, lk2, subln_g, lambda_init):
    b, s, _ = q.shape
    q = q.reshape(b, s, DIFF_HEADS, 2, DIFF_HEAD_DIM)
    k = k.reshape(b, s, DIFF_HEADS, 2, DIFF_HEAD_DIM)
    v = v.reshape(b, s, DIFF_HEADS, 2 * DIFF_HEAD_DIM)
    q1, q2 = q[..., 0, :], q[..., 1, :]
    k1, k2 = k[..., 0, :], k[..., 1, :]
    lam = (jnp.exp(jnp.sum(lq1.astype(jnp.float32) * lk1.astype(jnp.float32)))
           - jnp.exp(jnp.sum(lq2.astype(jnp.float32) * lk2.astype(jnp.float32)))
           + lambda_init)
    slopes = 2.0 ** (-8.0 * jnp.arange(1, DIFF_HEADS + 1, dtype=jnp.float32) / DIFF_HEADS)
    scale = DIFF_HEAD_DIM ** -0.5
    pos_q = jnp.broadcast_to(pos[None, :], (b, s))

    def block(q1b, q2b, pb):
        dist = jnp.abs(pb[:, :, None] - pos[None, None, :]).astype(jnp.float32)
        bias = -slopes[None, :, None, None] * dist[:, None, :, :]
        s1 = jnp.einsum('bqhd,bkhd->bhqk', q1b, k1).astype(jnp.float32) * scale + bias
        s2 = jnp.einsum('bqhd,bkhd->bhqk', q2b, k2).astype(jnp.float32) * scale + bias
        a = (jax.nn.softmax(s1, axis=-1) - lam * jax.nn.softmax(s2, axis=-1)).astype(v.dtype)
        return jnp.einsum('bhqk,bkhd->bqhd', a, v)

    o = sweep_query_blocks(block, q1, q2, pos_q)
    o = rms_norm(o, subln_g) * (1.0 - lambda_init)
    return o.reshape(b, s, DIFF_HEADS * 2 * DIFF_HEAD_DIM)

def setup_inputs(seed: int = 0) -> dict:
    key = jax.random.key(seed)
    ks = jax.random.split(key, 32)
    L, D, F = DEPTH, D_MODEL, D_FF
    f32 = jnp.float32

    def w(k, shape, fan_in, gain=1.0):
        return jax.random.normal(k, shape, f32) * (gain * fan_in ** -0.5)

    def gain(k, shape):
        return 1.0 + 0.02 * jax.random.normal(k, shape, f32)

    def bias(k, shape):
        return 0.02 * jax.random.normal(k, shape, f32)

    return {
        "x": jax.random.normal(ks[0], (BATCH, SEQ, D), f32),
        "ffn1_w_gate": w(ks[1], (L, D, F), D),
        "ffn1_w_up": w(ks[2], (L, D, F), D),
        "ffn1_w_down": w(ks[3], (L, F, D), F, DEEPNORM_BETA),
        "ln1_g": gain(ks[4], (L, D)),
        "ln1_b": bias(ks[5], (L, D)),
        "w_in": w(ks[6], (L, D, IN_WIDTH), D),
        "q_norm_g": gain(ks[7], (L, MLA_Q_RANK)),
        "w_q_up": w(ks[8], (L, MLA_Q_RANK, MLA_HEADS * (MLA_NOPE_DIM + MLA_ROPE_DIM)), MLA_Q_RANK),
        "kv_norm_g": gain(ks[9], (L, MLA_KV_RANK)),
        "w_kv_up": w(ks[10], (L, MLA_KV_RANK, MLA_HEADS * (MLA_NOPE_DIM + MLA_V_DIM)), MLA_KV_RANK),
        "diff_lambda_q1": 0.1 * jax.random.normal(ks[11], (L, DIFF_HEAD_DIM), f32),
        "diff_lambda_k1": 0.1 * jax.random.normal(ks[12], (L, DIFF_HEAD_DIM), f32),
        "diff_lambda_q2": 0.1 * jax.random.normal(ks[13], (L, DIFF_HEAD_DIM), f32),
        "diff_lambda_k2": 0.1 * jax.random.normal(ks[14], (L, DIFF_HEAD_DIM), f32),
        "diff_subln_g": gain(ks[15], (L, 2 * DIFF_HEAD_DIM)),
        "w_out": w(ks[16], (L, MIX_WIDTH, D), MIX_WIDTH, DEEPNORM_BETA),
        "ln2_g": gain(ks[17], (L, D)),
        "ln2_b": bias(ks[18], (L, D)),
        "ffn2_w_gate": w(ks[19], (L, D, F), D),
        "ffn2_w_up": w(ks[20], (L, D, F), D),
        "ffn2_w_down": w(ks[21], (L, F, D), F, DEEPNORM_BETA),
        "ln3_g": gain(ks[22], (L, D)),
        "ln3_b": bias(ks[23], (L, D)),
    }

def reference(x, ffn1_w_gate, ffn1_w_up, ffn1_w_down, ln1_g, ln1_b, w_in, q_norm_g, w_q_up,
              kv_norm_g, w_kv_up, diff_lambda_q1, diff_lambda_k1, diff_lambda_q2, diff_lambda_k2,
              diff_subln_g, w_out, ln2_g, ln2_b, ffn2_w_gate, ffn2_w_up, ffn2_w_down, ln3_g, ln3_b):
    s = x.shape[1]
    pos = jnp.arange(s, dtype=jnp.int32)
    split_idx = [int(i) for i in np.cumsum(IN_SPLITS)[:-1]]
    for l in range(DEPTH):
        lambda_init = 0.8 - 0.6 * math.exp(-0.3 * l)
        x = layer_norm(DEEPNORM_ALPHA * x + 0.5 * swiglu(x, ffn1_w_gate[l], ffn1_w_up[l], ffn1_w_down[l]),
                       ln1_g[l], ln1_b[l])
        h = x @ w_in[l]
        c_q, c_kv, k_rope, dq, dk, dv = jnp.split(h, split_idx, axis=-1)
        o_mla = mla_mixer(c_q, c_kv, k_rope, pos, q_norm_g[l], w_q_up[l], kv_norm_g[l], w_kv_up[l])
        o_diff = diff_mixer(dq, dk, dv, pos, diff_lambda_q1[l], diff_lambda_k1[l], diff_lambda_q2[l],
                            diff_lambda_k2[l], diff_subln_g[l], lambda_init)
        mix = jnp.concatenate([o_mla, o_diff], axis=-1) @ w_out[l]
        x = layer_norm(DEEPNORM_ALPHA * x + mix, ln2_g[l], ln2_b[l])
        x = layer_norm(DEEPNORM_ALPHA * x + 0.5 * swiglu(x, ffn2_w_gate[l], ffn2_w_up[l], ffn2_w_down[l]),
                       ln3_g[l], ln3_b[l])
    return x


_drawn_inputs = setup_inputs


def setup_inputs(seed=0):
    import zlib

    import numpy as np

    out = dict(_drawn_inputs(seed))
    spreads = {}
    factors = {'q_norm_g': 8.0,
     'kv_norm_g': 8.0,
     'diff_lambda_q1': 4.103,
     'diff_lambda_k1': 3.47,
     'diff_lambda_q2': 4.913,
     'diff_lambda_k2': 5.166,
     'diff_subln_g': 8.0}
    for name, (base, spread) in spreads.items():
        noise = np.random.default_rng([zlib.crc32(name.encode()), seed]).standard_normal(out[name].shape)
        drawn = base * np.exp(spread * noise) if base else spread * noise
        out[name] = __import__('jax').numpy.asarray(drawn.astype(out[name].dtype))
    for name, factor in factors.items():
        out[name] = (out[name] * factor).astype(out[name].dtype)
    return out
```

```python
from contextlib import ExitStack

import numpy as np
import concourse.bass as bass
from concourse import mybir

F32 = mybir.dt.float32
F32R = mybir.dt.float32r
ALU = mybir.AluOpType
ACT = mybir.ActivationFunctionType
AX = mybir.AxisListType

P = 128
D = 1024
S = 512
DEPTH = 2
F = 2816
HEADS = 4
NOPE, ROPE, VD = 128, 64, 128
QR, KVR = 256, 128
DH = 64
LAT = QR + KVR + ROPE
DQ0 = LAT
DK0 = DQ0 + HEADS * 2 * DH
DV0 = DK0 + HEADS * 2 * DH
EPS = 1e-5
ALPHA = (2 * DEPTH) ** 0.25
LN_EPS = EPS / ALPHA ** 2
KB = D // P
TT = S // P
FR = F // (2 * P)
UNITS = 6
RAW = 3
BANKS = 4
RG = (2, 2, 1, 1, 1, 1)
RG0 = (0, 2, 4, 5, 6, 7)
ROUNDS = 2 * FR + 1 + HEADS
LNS = 3
MLA_SCALE = (NOPE + ROPE) ** -0.5
DIFF_SCALE = DH ** -0.5
DIST = S + S - P
HALF = S // 2


def build(nc, x, g1, u1, d1, ln1_g, ln1_b, w_in, q_norm_g, w_q_up, kv_norm_g, w_kv_up, lq1, lk1, lq2, lk2,
          subln_g, w_out, ln2_g, ln2_b, g2, u2, d2, ln3_g, ln3_b, c_ident, c_dist, c_cos, c_sin, c_lam, out):
    ctx = ExitStack()
    with ctx:
        def sem(name):
            return ctx.enter_context(nc.semaphore(name))

        slab_bytes = nc.sbuf_usable_end - nc.sbuf_base - 64
        base = (nc.sbuf_base + 63) // 32 * 32
        ctx.enter_context(nc.sbuf_tensor("slab", [P, slab_bytes // 4 - 8], F32))
        top = [base]

        def size(shape):
            return int(np.prod(shape[1:])) * 4

        def at(offset, name, shape, dt=F32):
            assert offset + size(shape) <= base + slab_bytes, (name, offset + size(shape) - base - slab_bytes)
            return nc.alloc_sbuf_tensor_at(name, list(shape), dt, offset=offset)

        def sb(name, shape, dt=F32):
            t = at(top[0], name, shape, dt)
            top[0] += (size(shape) + 31) // 32 * 32
            return t

        def shared(*groups):
            start, end, made = top[0], top[0], []
            for group in groups:
                top[0] = start
                made += [sb(*one) for one in group]
                end = max(end, top[0])
            top[0] = end
            return made

        x_tok = sb("x_tok", [P, TT, D])
        x_hi = sb("x_hi", [P, KB, S], F32R)
        x_lo = sb("x_lo", [P, KB, S], F32R)
        raw = sb("raw", [P, RAW, D])
        w_hi = sb("w_hi", [P, UNITS, D], F32R)
        w_lo = sb("w_lo", [P, UNITS, D], F32R)
        (qd_hi, qd_lo, vd_hi, vd_lo, qn_hi, qn_lo, kn_hi, kn_lo, vm_hi, vm_lo,
         silu, prod, h_hi, h_lo) = shared(
            [(n, [P, S], F32R) for n in ("qd_hi", "qd_lo", "vd_hi", "vd_lo", "qn_hi", "qn_lo",
                                         "kn_hi", "kn_lo", "vm_hi", "vm_lo")],
            [("silu", [P, 2, S], F32), ("prod", [P, 2, S], F32),
             ("h_hi", [P, 2, S], F32R), ("h_lo", [P, 2, S], F32R)])
        kd_hi = sb("kd_hi", [P, 2, S], F32R)
        kd_lo = sb("kd_lo", [P, 2, S], F32R)
        qr_hi = sb("qr_hi", [P, S], F32R)
        qr_lo = sb("qr_lo", [P, S], F32R)
        kr_hi = sb("kr_hi", [P, S], F32R)
        kr_lo = sb("kr_lo", [P, S], F32R)
        c_hi, c_lo, ln_gb = shared([("c_hi", [P, 3, S], F32R), ("c_lo", [P, 3, S], F32R)],
                                   [("ln_gb", [P, 2, D], F32)])
        prb, c_tok, junk, lam_in, lam_junk = shared(
            [("prb", [P, 4, S], F32)],
            [("c_tok", [P, TT, LAT], F32), ("junk", [P, QR + KVR], F32)],
            [("lam_in", [P, 4, DH], F32), ("lam_junk", [P, 2, DH], F32)])
        a_hi = sb("a_hi", [P, 2, TT, HALF], F32R)
        a_lo = sb("a_lo", [P, 2, TT, HALF], F32R)
        od_hi = sb("od_hi", [P, S], F32R)
        od_lo = sb("od_lo", [P, S], F32R)
        om_hi = sb("om_hi", [P, S], F32R)
        om_lo = sb("om_lo", [P, S], F32R)
        od, sq, rb, rope_u, rope_w, lat_g = shared(
            [("od", [P, S], F32), ("sq", [P, S], F32), ("rb", [P, TT, P], F32)],
            [("rope_u", [P, S], F32), ("rope_w", [P, S], F32)],
            [("lat_g", [P, QR + KVR], F32)])
        dist = sb("dist", [P, DIST])
        alibi = sb("alibi", [P, DIST])
        cos = sb("cos", [P, S])
        sin = sb("sin", [P, S])
        ident = sb("ident", [P, P])
        lam_k = sb("lam_k", [P, 2])
        sub_g = sb("sub_g", [P, 1])
        sub_gs = sb("sub_gs", [P, 1])
        dots = sb("dots", [P, 2])
        edots = sb("edots", [P, 2])
        nlam = sb("nlam", [P, 2])
        ones = sb("ones", [P, 1])
        mhalf = sb("mhalf", [P, 8])
        wait_seat = sb("wait_seat", [P, 1])
        minus = sb("minus", [P, 1])
        ln_eps = sb("ln_eps", [P, 1])
        eps8 = sb("eps8", [P, 8])
        lat_n = sb("lat_n", [P, 8])
        nmean = sb("nmean", [P, TT])
        stats = sb("stats", [P, TT, 12])
        mv = sb("mv", [P, TT, 2])
        ve = sb("ve", [P, TT])
        rstd = sb("rstd", [P, TT])
        nmr = sb("nmr", [P, TT])
        ss = sb("ss", [P, 8])
        ssv = sb("ssv", [P, 8])
        rc = sb("rc", [P, 8])
        dmax = sb("dmax", [P, TT, 2])
        dneg = sb("dneg", [P, TT, 2])
        dsum = sb("dsum", [P, TT, 2])
        drec = sb("drec", [P, TT, 2])
        drl = sb("drl", [P, TT])
        mmax = sb("mmax", [P, TT])
        mneg = sb("mneg", [P, TT])
        msum = sb("msum", [P, TT])
        mrec = sb("mrec", [P, TT])
        ms = sb("ms", [P, TT])
        rms = sb("rms", [P, TT])

        ps = ctx.enter_context(nc.psum_tensor("ps", [P, 8, S], F32))

        const_landed = sem("const_landed")
        ident_landed = sem("ident_landed")
        x_landed = sem("x_landed")
        param_landed = sem("param_landed")
        gb_landed = sem("gb_landed")
        landed = [sem(f"landed{s}") for s in range(UNITS)]
        kvup_landed = sem("kvup_landed")
        stored = sem("stored")
        hi_done = sem("hi_done")
        lo_done = sem("lo_done")
        unit_used = sem("unit_used")
        prepared = sem("prepared")
        silu_done, prod_done = sem("silu_done"), sem("prod_done")
        h_hi_done, h_lo_done = sem("h_hi_done"), sem("h_lo_done")
        down_out, down_added = sem("down_out"), sem("down_added")
        ln_stat, ln_agg, ln_pool = sem("ln_stat"), sem("ln_agg"), sem("ln_pool")
        ln_norm, ln_scaled = sem("ln_norm"), sem("ln_scaled")
        xt_out, xt_hi_done, xt_lo_done = sem("xt_out"), sem("xt_hi_done"), sem("xt_lo_done")
        lat_out, lat_sq, lat_pool, lat_scaled = sem("lat_out"), sem("lat_sq"), sem("lat_pool"), sem("lat_scaled")
        latT_out, latT_hi, latT_lo = sem("latT_out"), sem("latT_hi"), sem("latT_lo")
        rope_step = sem("rope_step")
        lam_dot, lam_exp, lam_step = sem("lam_dot"), sem("lam_exp"), sem("lam_step")
        alibi_set = sem("alibi_set")
        proj_out, proj_hi, proj_lo = sem("proj_out"), sem("proj_hi"), sem("proj_lo")
        dscore, dbias, dneg_done, dexp, dnorm = (sem("dscore"), sem("dbias"), sem("dneg_done"), sem("dexp"),
                                                 sem("dnorm"))
        mscore, mmax_done, mneg_done, mexp, mnorm = (sem("mscore"), sem("mmax_done"), sem("mneg_done"),
                                                     sem("mexp"), sem("mnorm"))
        at_out, at_hi, at_lo = sem("at_out"), sem("at_hi"), sem("at_lo")
        pv_out = sem("pv_out")
        od_copied, sq_done, ms_out, ms_copied, rms_done = (sem("od_copied"), sem("sq_done"), sem("ms_out"),
                                                           sem("ms_copied"), sem("rms_done"))
        rb_done, rbT_out, od_scaled, od_hi_done, od_lo_done = (sem("rb_done"), sem("rbT_out"), sem("od_scaled"),
                                                               sem("od_hi_done"), sem("od_lo_done"))
        om_hi_done, om_lo_done = sem("om_hi_done"), sem("om_lo_done")
        wo_out, wo_added = sem("wo_out"), sem("wo_added")

        def raw32(t):
            return t.bitcast(F32)

        def rows(w):
            return w.rearrange("(k p) f -> p k f", p=P)

        LAT_W = [n * LAT for n in RG]
        HEAD_W = [D, D, D, 2 * (NOPE + ROPE) + NOPE + VD, D, D]
        MQ = NOPE + ROPE

        block = ctx.enter_context(nc.Block())

        @block.sync
        def _(sp):
            def unit(rnd, s, dst_w, src, shape=None):
                sp.wait_ge(lo_done, rnd * UNITS + (s + 1))
                dst = raw[:, s % RAW, 0:dst_w]
                if shape is not None:
                    dst = dst.rearrange("p (k f) -> p k f", k=shape)
                sp.dma_start(dst, src).then_inc(landed[s], 16)

            def ffn_loads(lay, base_rnd, wg, wu, wd):
                with sp.Fori(0, FR) as i:
                    rnd = sp.snap(lay * ROUNDS + base_rnd + i)
                    for j in range(2):
                        cols = bass.ds(i * (2 * P) + j * P, P)
                        unit(rnd, 2 * j, D, rows(wg[lay])[:, :, cols], KB)
                        unit(rnd, 2 * j + 1, D, rows(wu[lay])[:, :, cols], KB)
                    for j in range(2):
                        unit(rnd, 4 + j, D, wd[lay, bass.ds(i * (2 * P) + j * P, P), :])

            def gb_load(lay, g, b, free, count):
                sp.wait_ge(free, count)
                sp.dma_start(ln_gb[:, 0, :], g[lay].partition_broadcast(P)).then_inc(gb_landed, 16)
                sp.dma_start(ln_gb[:, 1, :], b[lay].partition_broadcast(P)).then_inc(gb_landed, 16)

            for t in range(TT):
                sp.dma_start(x_tok[:, t, :], x[0, t * P:(t + 1) * P, :]).then_inc(x_landed, 16)
            sp.dma_start(ident[:], c_ident).then_inc(ident_landed, 16)
            sp.dma_start(dist[:], c_dist).then_inc(const_landed, 16)
            sp.dma_start(cos[P // 2:, :], c_cos).then_inc(const_landed, 16)
            sp.dma_start(sin[P // 2:, :], c_sin).then_inc(const_landed, 16)
            with sp.Fori(0, DEPTH) as lay:
                sp.wait_ge(wo_added, lay * (HEADS * 2 * TT) + BANKS)
                sp.dma_start(lat_g[:, 0:QR], q_norm_g[lay].partition_broadcast(P)).then_inc(param_landed, 16)
                sp.dma_start(lat_g[:, QR:], kv_norm_g[lay].partition_broadcast(P)).then_inc(param_landed, 16)
                for n, v in enumerate((lq1, lk1, lq2, lk2)):
                    sp.dma_start(lam_in[:, n, :], v[lay].partition_broadcast(P)).then_inc(param_landed, 16)
                sp.dma_start(lam_k[:], c_lam[lay].partition_broadcast(P)).then_inc(param_landed, 16)
                sp.dma_start(sub_g[:], subln_g[lay].rearrange("(p a) -> p a", a=1)).then_inc(param_landed, 16)
                gb_load(lay, ln1_g, ln1_b, xt_lo_done, lay * (LNS * 2 * TT) + 2 * TT)
                ffn_loads(lay, 0, g1, u1, d1)
                rnd = sp.snap(lay * ROUNDS + FR)
                for s in range(UNITS):
                    src = rows(w_in[lay])[:, RG0[s]:RG0[s] + RG[s], 0:LAT]
                    unit(rnd, s, LAT_W[s], src, RG[s])
                with sp.Fori(0, HEADS) as h:
                    rnd = sp.snap(lay * ROUNDS + (FR + 1) + h)
                    for s, c0 in enumerate((DQ0, DK0, DV0)):
                        unit(rnd, s, D, rows(w_in[lay])[:, :, bass.ds(h * P + c0, P)], KB)
                    unit(rnd, 3, 2 * MQ, rows(w_q_up[lay])[:, :, bass.ds(h * MQ, MQ)], 2)
                    sp.dma_start(raw[:, 0, 2 * MQ:2 * MQ + NOPE + VD],
                                 w_kv_up[lay, :, bass.ds(h * (NOPE + VD), NOPE + VD)]).then_inc(kvup_landed, 16)
                    unit(rnd, 4, D, w_out[lay, bass.ds(h * P + HEADS * VD, P), :])
                    unit(rnd, 5, D, w_out[lay, bass.ds(h * P, P), :])
                gb_load(lay, ln2_g, ln2_b, proj_lo, (lay * HEADS + HEADS) * 8)
                ffn_loads(lay, FR + 1 + HEADS, g2, u2, d2)
                gb_load(lay, ln3_g, ln3_b, ln_scaled, (lay * LNS + 2) * (2 * TT))
            for t in range(TT):
                sp.wait_ge(ln_scaled, (DEPTH * LNS - 1) * 2 * TT + 2 * t + 2)
                sp.dma_start(out[0, t * P:(t + 1) * P, :], x_tok[:, t, :]).then_inc(stored, 16)
            sp.wait_ge(stored, 16 * TT)

        @block.gpsimd
        def _(pool):
            pool.memset(ones[:], 1.0).then_inc(prepared, 1)
            pool.memset(mhalf[:], -0.5).then_inc(prepared, 1)
            pool.memset(minus[:], -1.0).then_inc(prepared, 1)
            pool.memset(ln_eps[:], LN_EPS).then_inc(prepared, 1)
            pool.memset(eps8[:], EPS).then_inc(prepared, 1)
            pool.memset(lat_n[:, 0:TT], 1.0 / QR).then_inc(prepared, 1)
            pool.memset(lat_n[:, TT:], 1.0 / KVR).then_inc(prepared, 1)
            pool.sem_inc(lo_done, RAW)

            def lo_part(rnd, s, width):
                pool.wait_ge(hi_done, rnd * UNITS + (s + 1))
                pool.tensor_tensor(w_lo[:, s, 0:width], raw[:, s % RAW, 0:width], raw32(w_hi[:, s, 0:width]),
                                   ALU.subtract).then_inc(lo_done, 1)

            def ffn_split(lay, base_rnd):
                with pool.Fori(0, FR) as i:
                    rnd = pool.snap(lay * ROUNDS + base_rnd + i)
                    for s in range(UNITS):
                        lo_part(rnd, s, D)

            def ln_power(lay, w):
                ln = pool.snap(lay * LNS + w)
                for t in range(TT):
                    c = slice(t, t + 1)
                    pool.wait_ge(ln_agg, ln * TT + (t + 1))
                    pool.tensor_tensor(ve[:, c], mv[:, t, 1:2], ln_eps[:], ALU.add).then_inc(ln_pool, 1)
                    pool.tensor_tensor(nmean[:, c], mv[:, t, 0:1], minus[:], ALU.mult).then_inc(ln_pool, 1)
                    pool.wait_ge(ln_pool, ln * (4 * TT) + (4 * t + 2))
                    pool.tensor_tensor(rstd[:, c], ve[:, c], mhalf[:, 0:1], ALU.pow).then_inc(ln_pool, 1)
                    pool.wait_ge(ln_pool, ln * (4 * TT) + (4 * t + 3))
                    pool.tensor_tensor(nmr[:, c], nmean[:, c], rstd[:, c], ALU.mult).then_inc(ln_pool, 1)

            with pool.Fori(0, DEPTH) as lay:
                ffn_split(lay, 0)
                ln_power(lay, 0)
                rnd = pool.snap(lay * ROUNDS + FR)
                for s in range(UNITS):
                    lo_part(rnd, s, LAT_W[s])
                pool.wait_ge(lat_sq, (lay + 1) * (2 * TT))
                pool.tensor_tensor(ssv[:], ss[:], lat_n[:], ALU.mult).then_inc(lat_pool, 1)
                pool.wait_ge(lat_pool, lay * 3 + 1)
                pool.tensor_tensor(ssv[:], ssv[:], eps8[:], ALU.add).then_inc(lat_pool, 1)
                pool.wait_ge(lat_pool, lay * 3 + 2)
                pool.tensor_tensor(rc[:], ssv[:], mhalf[:], ALU.pow).then_inc(lat_pool, 1)
                with pool.Fori(0, HEADS) as h:
                    rnd = pool.snap(lay * ROUNDS + (FR + 1) + h)
                    for s in range(UNITS):
                        lo_part(rnd, s, HEAD_W[s])
                    pool.wait_ge(ms_copied, lay * HEADS + h + 1)
                    pool.tensor_tensor(rms[:], ms[:], mhalf[:, 0:TT], ALU.pow).then_inc(rms_done, 1)
                ln_power(lay, 1)
                ffn_split(lay, FR + 1 + HEADS)
                ln_power(lay, 2)

        @block.scalar
        def _(act):
            def hi_part(rnd, s, width, also=None):
                act.wait_ge(landed[s], rnd * 16 + 16)
                if also is not None:
                    act.wait_ge(*also)
                act.wait_ge(unit_used, rnd * UNITS + (s + 1))
                act.copy(w_hi[:, s, 0:width], raw[:, s % RAW, 0:width]).then_inc(hi_done, 1)

            def ffn_act(lay, which, base_rnd):
                with act.Fori(0, FR) as i:
                    rnd = act.snap(lay * ROUNDS + base_rnd + i)
                    ffn = act.snap(lay * (2 * FR) + which * FR + i)
                    for s in range(4):
                        hi_part(rnd, s, D)
                    for j in range(2):
                        act.wait_ge(unit_used, rnd * UNITS + (UNITS + 2 * j + 1))
                        act.activation(silu[:, j, :], ps[:, 2 * j, :], ACT.Silu).then_inc(silu_done, 1)
                        act.wait_ge(prod_done, ffn * 2 + (j + 1))
                        act.wait_ge(unit_used, rnd * UNITS + UNITS)
                        act.copy(h_hi[:, j, :], prod[:, j, :]).then_inc(h_hi_done, 1)
                        if j == 0:
                            hi_part(rnd, 4, D)
                            hi_part(rnd, 5, D)

            def turned_hi(epoch, t):
                for b in range(2):
                    act.wait_ge(xt_out, epoch * (2 * TT) + (2 * t + b + 1))
                    act.copy(x_hi[:, 4 * b:4 * b + 4, t * P:(t + 1) * P],
                             ps[:, 2 * t + b, :].rearrange("p (k q) -> p k q", k=4)).then_inc(xt_hi_done, 1)

            def norm(ln, t):
                act.wait_ge(ln_pool, ln * (4 * TT) + (4 * t + 4))
                act.activation(x_tok[:, t, :], x_tok[:, t, :], ACT.Identity, bias=nmr[:, t:t + 1],
                               scale=rstd[:, t:t + 1]).then_inc(ln_norm, 1)

            def ln_act(lay, w):
                ln = act.snap(lay * LNS + w)
                epoch = act.snap(ln + 1)
                norm(ln, 0)
                norm(ln, 1)
                for t in range(TT):
                    if t + 2 < TT:
                        norm(ln, t + 2)
                    turned_hi(epoch, t)

            act.sem_inc(mexp, BANKS)
            for t in range(TT):
                turned_hi(0, t)
            with act.Fori(0, DEPTH) as lay:
                act.wait_ge(lam_dot, lay * 2 + 2)
                act.activation(edots[:], dots[:], ACT.Exp).then_inc(lam_exp, 1)
                ffn_act(lay, 0, 0)
                ln_act(lay, 0)
                rnd = act.snap(lay * ROUNDS + FR)
                for s in range(UNITS):
                    hi_part(rnd, s, LAT_W[s])
                for t in range(TT):
                    if t < TT - 1:
                        act.wait_ge(lat_out, lay * (TT - 1) + (t + 1))
                    else:
                        act.wait_ge(unit_used, rnd * UNITS + 2 * UNITS)
                    if t > 0:
                        act.wait_ge(lat_sq, lay * (2 * TT) + 2 * t)
                    act.activation(junk[:, 0:QR], ps[:, t, 0:QR], ACT.Square,
                                   accum_out=ss[:, t:t + 1]).then_inc(lat_sq, 1)
                    act.activation(junk[:, QR:], ps[:, t, QR:QR + KVR], ACT.Square,
                                   accum_out=ss[:, TT + t:TT + t + 1]).then_inc(lat_sq, 1)
                for f in range(3):
                    act.wait_ge(latT_out, lay * 4 + (f + 1))
                    act.copy(c_hi[:, f, :], ps[:, 4 + f, :]).then_inc(latT_hi, 1)
                act.wait_ge(rope_step, lay * (4 * (HEADS + 1)) + 4)
                act.copy(kr_hi[P // 2:, :], rope_w[P // 2:, :]).then_inc(latT_hi, 1)
                with act.Fori(0, HEADS) as h:
                    rnd = act.snap(lay * ROUNDS + (FR + 1) + h)
                    hd = act.snap(lay * HEADS + h)
                    for s in range(4):
                        hi_part(rnd, s, HEAD_W[s], also=(kvup_landed, hd * 16 + 16) if s == 3 else None)

                    def unit_product(s):
                        act.wait_ge(unit_used, rnd * UNITS + (UNITS + s + 1))

                    def proj(dst, src):
                        act.copy(dst, src).then_inc(proj_hi, 1)

                    unit_product(0)
                    proj(qd_hi[:], ps[:, 0, :])
                    unit_product(1)
                    for m in range(2):
                        half = slice(m * DH, (m + 1) * DH)
                        proj(kd_hi[half, m, :], ps[half, 1, :])
                    unit_product(2)
                    proj(vd_hi[:], ps[:, 0, :])
                    hi_part(rnd, 4, D)
                    hi_part(rnd, 5, D)
                    act.wait_ge(proj_out, hd * 3 + 1)
                    proj(qn_hi[:], ps[:, 1, :])
                    act.wait_ge(rope_step, lay * (4 * (HEADS + 1)) + h * 4 + 8)
                    proj(qr_hi[P // 2:, :], rope_w[P // 2:, :])
                    act.wait_ge(proj_out, hd * 3 + 3)
                    proj(kn_hi[:], ps[:, 1, :])
                    unit_product(3)
                    proj(vm_hi[:], ps[:, 0, :])

                    def a_part(n, t):
                        act.wait_ge(at_out, hd * (2 * TT) + (n + 1))
                        if n % 2 == 0:
                            act.wait_ge(pv_out, hd * 4 + (n // 2 + 1))
                        act.copy(a_hi[:, n // 2 % 2, :, (n % 2) * P:(n % 2 + 1) * P],
                                 ps[:, 6 + n % 2, :].rearrange("p (j q) -> p j q", j=TT)).then_inc(at_hi, 1)

                    def d_exp(t):
                        act.wait_ge(dneg_done, hd * TT + (t + 1))
                        for m in range(2):
                            p = prb[:, 2 * (t % 2) + m, :]
                            act.activation(p, p, ACT.Exp, bias=dneg[:, t, m:m + 1],
                                           accum_out=dsum[:, t, m:m + 1]).then_inc(dexp, 1)

                    def m_exp(t):
                        act.wait_ge(mneg_done, hd * TT + (t + 1))
                        act.wait_ge(at_out, hd * (2 * TT) + (3 + t // 2))
                        act.activation(prb[:, t, :], ps[:, 2 + t, :], ACT.Exp, bias=mneg[:, t:t + 1],
                                       scale=MLA_SCALE, accum_out=msum[:, t:t + 1]).then_inc(mexp, 1)

                    d_exp(0)
                    d_exp(1)
                    for t in range(TT):
                        a_part(t, t)
                        if t + 2 < TT:
                            d_exp(t + 2)
                    m_exp(0)
                    act.wait_ge(od_copied, hd + 1)
                    act.activation(sq[:], od[:], ACT.Square).then_inc(sq_done, 1)
                    m_exp(1)
                    for t in range(TT):
                        a_part(4 + t, t)
                        if t + 2 < TT:
                            m_exp(t + 2)
                    act.wait_ge(od_scaled, hd + 1)
                    act.copy(od_hi[:], od[:]).then_inc(od_hi_done, 1)
                    act.wait_ge(pv_out, hd * 4 + (2 + 4))
                    act.copy(om_hi[:], ps[:, 0, :]).then_inc(om_hi_done, 1)
                ln_act(lay, 1)
                ffn_act(lay, 1, FR + 1 + HEADS)
                ln_act(lay, 2)

        @block.vector
        def _(dve):
            def rest(lo, src, hi):
                return dve.tensor_tensor(lo, src, raw32(hi), ALU.subtract)

            def turned_lo(epoch, t):
                for b in range(2):
                    dve.wait_ge(xt_hi_done, epoch * (2 * TT) + (2 * t + b + 1))
                    k, q = slice(4 * b, 4 * b + 4), slice(t * P, (t + 1) * P)
                    rest(x_lo[:, k, q], ps[:, 2 * t + b, :].rearrange("p (k q) -> p k q", k=4),
                         x_hi[:, k, q]).then_inc(xt_lo_done, 1)

            def ffn_dve(lay, which):
                with dve.Fori(0, FR) as i:
                    rnd = dve.snap(lay * ROUNDS + (which * (FR + 1 + HEADS)) + i)
                    ffn = dve.snap(lay * (2 * FR) + which * FR + i)
                    for j in range(2):
                        dve.wait_ge(silu_done, ffn * 2 + (j + 1))
                        dve.wait_ge(unit_used, rnd * UNITS + (UNITS + 2 * j + 2))
                        dve.tensor_tensor(prod[:, j, :], ps[:, 2 * j + 1, :], silu[:, j, :], ALU.mult)\
                            .then_inc(prod_done, 1)
                        dve.wait_ge(h_hi_done, ffn * 2 + (j + 1))
                        rest(h_lo[:, j, :], prod[:, j, :], h_hi[:, j, :]).then_inc(h_lo_done, 1)
                    dve.wait_ge(down_added, ffn * (2 * TT) + BANKS)
                    for b in range(2 * TT):
                        xs = x_tok[:, b // 2, (b % 2) * S:(b % 2 + 1) * S]
                        if b < 2 * TT - 1:
                            dve.wait_ge(down_out, ffn * (2 * TT - 1) + (b + 1))
                        else:
                            dve.wait_ge(unit_used, rnd * UNITS + 2 * UNITS)
                        dve.scalar_tensor_tensor(xs, ps[:, 4 + b % 4, :], 0.5 / ALPHA, xs, ALU.mult, ALU.add)\
                            .then_inc(down_added, 1)

            def ln_dve(lay, w, added, count):
                ln = dve.snap(lay * LNS + w)
                epoch = dve.snap(ln + 1)
                dve.wait_ge(added, count)

                def stat(t):
                    for b in range(2):
                        dve.bn_stats(stats[:, t, 6 * b:6 * b + 6], x_tok[:, t, b * S:(b + 1) * S])\
                            .then_inc(ln_stat, 1)
                    dve.wait_ge(ln_stat, ln * (2 * TT) + (2 * t + 2))
                    dve.memset(wait_seat[:], 0.0)
                    dve.bn_aggr(mv[:, t, :], stats[:, t, :]).then_inc(ln_agg, 1)

                def gain(t):
                    dve.wait_ge(ln_norm, ln * TT + (t + 1))
                    if t == 0:
                        dve.wait_ge(gb_landed, ln * 32 + 32)
                    xs = x_tok[:, t, :]
                    dve.tensor_tensor(xs, xs, ln_gb[:, 0, :], ALU.mult).then_inc(ln_scaled, 1)
                    dve.wait_ge(ln_scaled, ln * (2 * TT) + (2 * t + 1))
                    dve.tensor_tensor(xs, xs, ln_gb[:, 1, :], ALU.add).then_inc(ln_scaled, 1)

                stat(0)
                stat(1)
                gain(0)
                stat(2)
                gain(1)
                turned_lo(epoch, 0)
                stat(3)
                gain(2)
                turned_lo(epoch, 1)
                gain(3)
                turned_lo(epoch, 2)
                turned_lo(epoch, 3)

            def rope(index, bank):
                a, b = slice(P // 2, P // 2 + ROPE // 2), slice(P // 2 + ROPE // 2, P)
                both = slice(P // 2, P)
                dve.tensor_tensor(rope_u[a, :], ps[b, bank, :], sin[b, :], ALU.mult).then_inc(rope_step, 1)
                dve.tensor_tensor(rope_u[b, :], ps[a, bank, :], sin[a, :], ALU.mult).then_inc(rope_step, 1)
                dve.tensor_tensor(rope_w[both, :], ps[both, bank, :], cos[both, :], ALU.mult)\
                    .then_inc(rope_step, 1)
                dve.wait_ge(rope_step, index * 4 + 3)
                dve.tensor_tensor(rope_w[both, :], rope_w[both, :], rope_u[both, :], ALU.add)\
                    .then_inc(rope_step, 1)

            dve.sem_inc(down_added, BANKS)
            dve.sem_inc(wo_added, BANKS)
            for z in (kd_hi, kd_lo):
                dve.memset(raw32(z[P // 2:P, 0, :]), 0.0).then_inc(prepared, 1)
                dve.memset(raw32(z[0:P // 2, 1, :]), 0.0).then_inc(prepared, 1)
            for z in (qr_hi, qr_lo, kr_hi, kr_lo):
                dve.memset(raw32(z[0:P // 2, :]), 0.0).then_inc(prepared, 1)
            for t in range(TT):
                turned_lo(0, t)
            dve.wait_ge(const_landed, 48)
            with dve.Fori(0, DEPTH) as lay:
                dve.wait_ge(param_landed, lay * 128 + 128)
                for n in range(2):
                    dve.tensor_tensor_reduce(lam_junk[:, n, :], lam_in[:, 2 * n, :], lam_in[:, 2 * n + 1, :], 1.0, 0.0,
                                             ALU.mult, ALU.add, dots[:, n:n + 1]).then_inc(lam_dot, 1)
                dve.tensor_tensor(sub_gs[:], sub_g[:], lam_k[:, 1:2], ALU.mult).then_inc(lam_step, 1)
                dve.wait_ge(lam_exp, lay + 1)
                dve.tensor_tensor(nlam[:, 0:1], edots[:, 1:2], edots[:, 0:1], ALU.subtract).then_inc(lam_step, 1)
                dve.wait_ge(lam_step, lay * 3 + 2)
                dve.tensor_tensor(nlam[:, 1:2], nlam[:, 0:1], lam_k[:, 0:1], ALU.subtract).then_inc(lam_step, 1)
                ffn_dve(lay, 0)
                ln_dve(lay, 0, down_added, (lay * 2 + 1) * (FR * 2 * TT) + BANKS)
                dve.wait_ge(lat_pool, lay * 3 + 3)
                for t in range(TT):
                    dve.scalar_tensor_tensor(c_tok[:, t, 0:QR], ps[:, t, 0:QR], rc[:, t:t + 1], lat_g[:, 0:QR],
                                             ALU.mult, ALU.mult).then_inc(lat_scaled, 1)
                    dve.scalar_tensor_tensor(c_tok[:, t, QR:QR + KVR], ps[:, t, QR:QR + KVR],
                                             rc[:, TT + t:TT + t + 1], lat_g[:, QR:], ALU.mult, ALU.mult)\
                        .then_inc(lat_scaled, 1)
                    dve.tensor_copy(c_tok[:, t, QR + KVR:], ps[:, t, QR + KVR:LAT]).then_inc(lat_scaled, 1)
                for f in range(3):
                    dve.wait_ge(latT_hi, lay * 4 + (f + 1))
                    rest(c_lo[:, f, :], ps[:, 4 + f, :], c_hi[:, f, :]).then_inc(latT_lo, 1)
                dve.wait_ge(latT_out, lay * 4 + 4)
                rope(lay * (HEADS + 1), 7)
                dve.wait_ge(latT_hi, lay * 4 + 4)
                rest(kr_lo[P // 2:, :], rope_w[P // 2:, :], kr_hi[P // 2:, :]).then_inc(latT_lo, 1)
                dve.tensor_scalar(alibi[:], dist[:], -1.0 / DIFF_SCALE, None, ALU.mult).then_inc(alibi_set, 1)
                with dve.Fori(0, HEADS) as h:
                    rnd = dve.snap(lay * ROUNDS + (FR + 1) + h)
                    hd = dve.snap(lay * HEADS + h)
                    dve.wait_ge(alibi_set, lay * (HEADS + 1) + h + 1)
                    dve.tensor_scalar(alibi[:], alibi[:], 0.25, None, ALU.mult).then_inc(alibi_set, 1)

                    def proj(n_hi, lo, src, hi):
                        dve.wait_ge(proj_hi, hd * 8 + n_hi)
                        rest(lo, src, hi).then_inc(proj_lo, 1)

                    proj(1, qd_lo[:], ps[:, 0, :], qd_hi[:])
                    for m in range(2):
                        half = slice(m * DH, (m + 1) * DH)
                        proj(2 + m, kd_lo[half, m, :], ps[half, 1, :], kd_hi[half, m, :])
                    proj(4, vd_lo[:], ps[:, 0, :], vd_hi[:])
                    proj(5, qn_lo[:], ps[:, 1, :], qn_hi[:])
                    dve.wait_ge(proj_out, hd * 3 + 2)
                    rope(lay * (HEADS + 1) + h + 1, 0)
                    proj(6, qr_lo[P // 2:, :], rope_w[P // 2:, :], qr_hi[P // 2:, :])
                    proj(7, kn_lo[:], ps[:, 1, :], kn_hi[:])
                    proj(8, vm_lo[:], ps[:, 0, :], vm_hi[:])

                    def d_bias(t):
                        if t >= 2:
                            dve.wait_ge(at_out, hd * (2 * TT) + (t - 1))
                        if t == 0:
                            dve.wait_ge(alibi_set, lay * (HEADS + 1) + h + 2)
                        dve.wait_ge(dscore, hd * (2 * TT) + (2 * t + 2))
                        dve.memset(wait_seat[:], 0.0)
                        for m in range(2):
                            off = (TT - 1 - t) * P
                            dve.tensor_tensor_reduce(prb[:, 2 * (t % 2) + m, :], ps[:, 2 + (2 * t + m) % 4, :],
                                                     alibi[:, off:off + S], DIFF_SCALE, -3.0e38, ALU.add, ALU.max,
                                                     dmax[:, t, m:m + 1]).then_inc(dbias, 1)
                        dve.wait_ge(dbias, hd * (2 * TT) + (2 * t + 2))
                        dve.tensor_scalar(dneg[:, t, :], dmax[:, t, :], -1.0, None, ALU.mult)\
                            .then_inc(dneg_done, 1)

                    def d_norm(t):
                        p1, p2 = prb[:, 2 * (t % 2), :], prb[:, 2 * (t % 2) + 1, :]
                        dve.wait_ge(dexp, hd * (2 * TT) + (2 * t + 2))
                        dve.reciprocal(drec[:, t, :], dsum[:, t, :]).then_inc(dnorm, 1)
                        dve.wait_ge(dnorm, hd * (4 * TT) + (4 * t + 1))
                        dve.tensor_scalar(drl[:, t:t + 1], drec[:, t, 1:2], nlam[:, 1:2], None, ALU.mult)\
                            .then_inc(dnorm, 1)
                        dve.tensor_scalar(p1, p1, drec[:, t, 0:1], None, ALU.mult).then_inc(dnorm, 1)
                        dve.wait_ge(dnorm, hd * (4 * TT) + (4 * t + 3))
                        dve.scalar_tensor_tensor(p1, p2, drl[:, t:t + 1], p1, ALU.mult, ALU.add)\
                            .then_inc(dnorm, 1)

                    def a_rest(n):
                        dve.wait_ge(at_hi, hd * (2 * TT) + (n + 1))
                        q = slice((n % 2) * P, (n % 2 + 1) * P)
                        rest(a_lo[:, n // 2 % 2, :, q], ps[:, 6 + n % 2, :].rearrange("p (j q) -> p j q", j=TT),
                             a_hi[:, n // 2 % 2, :, q]).then_inc(at_lo, 1)

                    def m_max(t):
                        dve.wait_ge(mscore, hd * TT + (t + 1))
                        dve.tensor_reduce(mmax[:, t:t + 1], ps[:, 2 + t, :], AX.X, ALU.max)\
                            .then_inc(mmax_done, 1)
                        dve.wait_ge(mmax_done, hd * TT + (t + 1))
                        dve.tensor_scalar(mneg[:, t:t + 1], mmax[:, t:t + 1], -MLA_SCALE, None, ALU.mult)\
                            .then_inc(mneg_done, 1)

                    def m_norm(t):
                        dve.wait_ge(mexp, hd * TT + (BANKS + t + 1))
                        dve.reciprocal(mrec[:, t:t + 1], msum[:, t:t + 1]).then_inc(mnorm, 1)
                        dve.wait_ge(mnorm, hd * (2 * TT) + (2 * t + 1))
                        dve.tensor_scalar(prb[:, t, :], prb[:, t, :], mrec[:, t:t + 1], None, ALU.mult)\
                            .then_inc(mnorm, 1)

                    d_bias(0)
                    d_bias(1)
                    d_norm(0)
                    d_bias(2)
                    d_norm(1)
                    a_rest(0)
                    d_bias(3)
                    d_norm(2)
                    a_rest(1)
                    d_norm(3)
                    a_rest(2)
                    a_rest(3)
                    m_max(0)
                    m_max(1)
                    dve.wait_ge(pv_out, hd * 4 + (2 + 2))
                    dve.tensor_copy(od[:], ps[:, 1, :]).then_inc(od_copied, 1)
                    m_norm(0)
                    m_max(2)
                    m_norm(1)
                    dve.wait_ge(ms_out, hd + 1)
                    dve.tensor_scalar(ms[:], ps[:, 1, 0:TT], 1.0 / (2 * DH), EPS, ALU.mult, ALU.add)\
                        .then_inc(ms_copied, 1)
                    a_rest(4)
                    m_max(3)
                    m_norm(2)
                    a_rest(5)
                    dve.wait_ge(rms_done, hd + 1)
                    dve.tensor_copy(rb[:], rms[:].rearrange("p (t a) -> p t a", a=1).to_broadcast([P, TT, P]))\
                        .then_inc(rb_done, 1)
                    m_norm(3)
                    a_rest(6)
                    a_rest(7)
                    dve.wait_ge(rbT_out, hd + 1)
                    dve.scalar_tensor_tensor(od[:], ps[:, 1, :], sub_gs[:], od[:], ALU.mult, ALU.mult)\
                        .then_inc(od_scaled, 1)
                    dve.wait_ge(od_hi_done, hd + 1)
                    rest(od_lo[:], od[:], od_hi[:]).then_inc(od_lo_done, 1)
                    dve.wait_ge(om_hi_done, hd + 1)
                    rest(om_lo[:], ps[:, 0, :], om_hi[:]).then_inc(om_lo_done, 1)
                    dve.wait_ge(wo_added, hd * (2 * TT) + BANKS)
                    for b in range(2 * TT):
                        xs = x_tok[:, b // 2, (b % 2) * S:(b % 2 + 1) * S]
                        if b < 2 * TT - 1:
                            dve.wait_ge(wo_out, hd * (2 * TT - 1) + (b + 1))
                        else:
                            dve.wait_ge(unit_used, rnd * UNITS + 2 * UNITS)
                        dve.scalar_tensor_tensor(xs, ps[:, 4 + b % 4, :], 1.0 / ALPHA, xs, ALU.mult, ALU.add)\
                            .then_inc(wo_added, 1)
                ln_dve(lay, 1, wo_added, (lay + 1) * (HEADS * 2 * TT) + BANKS)
                ffn_dve(lay, 1)
                ln_dve(lay, 2, down_added, (lay * 2 + 2) * (FR * 2 * TT) + BANKS)

        @block.tensor
        def _(pe):
            pe.sem_inc(unit_used, UNITS)
            pe.sem_inc(pv_out, 2)

            def product(out, left, right, first, last):
                pe.matmul(out, left[0], right[0], start=first, stop=False)
                pe.matmul(out, left[0], right[1], start=False, stop=False)
                return pe.matmul(out, left[1], right[0], start=False, stop=last)

            def split_unit(rnd, s):
                pe.wait_ge(lo_done, rnd * UNITS + (RAW + s + 1))

            def w(s, cols):
                return w_hi[:, s, cols], w_lo[:, s, cols]

            def xt(k, q=slice(0, S)):
                return x_hi[:, k, q], x_lo[:, k, q]

            def turn_x(epoch, t):
                for b in range(2):
                    for k in range(4):
                        last = pe.transpose(ps[:, 2 * t + b, k * P:(k + 1) * P],
                                            x_tok[:, t, (4 * b + k) * P:(4 * b + k + 1) * P], ident[:])
                    last.then_inc(xt_out, 1)

            def ln_pe(lay, w_):
                ln = pe.snap(lay * LNS + w_)
                for t in range(TT):
                    pe.wait_ge(ln_scaled, ln * (2 * TT) + (2 * t + 2))
                    turn_x(ln, t)

            def add_rows(rnd, base_index, lefts, out_sem, added_sem):
                for b in range(2 * TT):
                    t, half = b // 2, slice((b % 2) * S, (b % 2 + 1) * S)
                    pe.wait_ge(added_sem, base_index + (b + 1))
                    tok = slice(t * P, (t + 1) * P)
                    for j in range(2):
                        hi, lo = lefts[j]
                        last = product(ps[:, 4 + b % 4, :], (hi[:, tok], lo[:, tok]), w(4 + j, half),
                                       j == 0, j == 1)
                        if b == 2 * TT - 1:
                            last.then_inc(unit_used, 1)
                        elif j == 1:
                            last.then_inc(out_sem, 1)

            def ffn_pe(lay, which, base_rnd):
                with pe.Fori(0, FR) as i:
                    rnd = pe.snap(lay * ROUNDS + base_rnd + i)
                    ffn = pe.snap(lay * (2 * FR) + which * FR + i)
                    pe.wait_ge(xt_lo_done, lay * (LNS * 2 * TT) + (which * 2 + 1) * (2 * TT))
                    for s in range(4):
                        split_unit(rnd, s)
                        for k in range(KB):
                            last = product(ps[:, s, :], w(s, slice(k * P, (k + 1) * P)), xt(k),
                                           k == 0, k == KB - 1)
                        last.then_inc(unit_used, 1)
                    split_unit(rnd, 4)
                    split_unit(rnd, 5)
                    pe.wait_ge(h_lo_done, ffn * 2 + 2)
                    add_rows(rnd, ffn * (2 * TT), [(h_hi[:, j, :], h_lo[:, j, :]) for j in range(2)],
                             down_out, down_added)

            pe.wait_ge(ident_landed, 16)
            pe.wait_ge(prepared, 15)
            pe.wait_ge(x_landed, 16 * TT)
            for t in range(TT):
                turn_x(0, t)
            with pe.Fori(0, DEPTH) as lay:
                ffn_pe(lay, 0, 0)
                ln_pe(lay, 0)
                rnd = pe.snap(lay * ROUNDS + FR)
                pe.wait_ge(xt_lo_done, lay * (LNS * 2 * TT) + 2 * (2 * TT))
                for s in range(UNITS):
                    split_unit(rnd, s)
                    for n in range(RG[s]):
                        k = RG0[s] + n
                        for t in range(TT):
                            last = product(ps[:, t, 0:LAT], xt(k, slice(t * P, (t + 1) * P)),
                                           w(s, slice(n * LAT, (n + 1) * LAT)), k == 0, k == KB - 1)
                            if k == KB - 1 and t < TT - 1:
                                last.then_inc(lat_out, 1)
                    last.then_inc(unit_used, 1)
                pe.wait_ge(lat_scaled, (lay + 1) * (3 * TT))
                for f, c0 in enumerate((0, P, 2 * P, LAT - P)):
                    for t in range(TT):
                        last = pe.transpose(ps[:, 4 + f, t * P:(t + 1) * P], c_tok[:, t, c0:c0 + P], ident[:])
                    last.then_inc(latT_out, 1)
                with pe.Fori(0, HEADS) as h:
                    rnd = pe.snap(lay * ROUNDS + (FR + 1) + h)
                    hd = pe.snap(lay * HEADS + h)

                    def bank_split(n):
                        pe.wait_ge(proj_lo, hd * 8 + n)

                    for s in range(2):
                        split_unit(rnd, s)
                        for k in range(KB):
                            last = product(ps[:, s, :], w(s, slice(k * P, (k + 1) * P)), xt(k),
                                           k == 0, k == KB - 1)
                        last.then_inc(unit_used, 1)
                    split_unit(rnd, 2)
                    bank_split(1)
                    for t in range(TT):
                        for k in range(KB):
                            last = product(ps[:, 0, t * P:(t + 1) * P], xt(k, slice(t * P, (t + 1) * P)),
                                           w(2, slice(k * P, (k + 1) * P)), k == 0, k == KB - 1)
                    last.then_inc(unit_used, 1)
                    split_unit(rnd, 3)
                    pe.wait_ge(latT_lo, lay * 4 + 4)
                    bank_split(3)
                    for k in range(2):
                        last = product(ps[:, 1, :], w(3, slice(k * MQ, k * MQ + NOPE)),
                                       (c_hi[:, k, :], c_lo[:, k, :]), k == 0, k == 1)
                    last.then_inc(proj_out, 1)
                    bank_split(4)
                    for k in range(2):
                        last = product(ps[:, 0, :], w(3, slice(k * MQ + MQ - P, (k + 1) * MQ)),
                                       (c_hi[:, k, :], c_lo[:, k, :]), k == 0, k == 1)
                    last.then_inc(proj_out, 1)
                    bank_split(5)
                    last = product(ps[:, 1, :], w(3, slice(2 * MQ, 2 * MQ + NOPE)),
                                   (c_hi[:, 2, :], c_lo[:, 2, :]), True, True)
                    last.then_inc(proj_out, 1)
                    bank_split(6)
                    for t in range(TT):
                        tok = slice(t * P, (t + 1) * P)
                        last = product(ps[:, 0, tok], (c_hi[:, 2, tok], c_lo[:, 2, tok]),
                                       w(3, slice(2 * MQ + NOPE, 2 * MQ + NOPE + VD)), True, True)
                    last.then_inc(unit_used, 1)

                    def d_scores(t):
                        tok = slice(t * P, (t + 1) * P)
                        for m in range(2):
                            if t >= 2:
                                pe.wait_ge(dbias, hd * (2 * TT) + (2 * t + m - 3))
                            product(ps[:, 2 + (2 * t + m) % 4, :], (qd_hi[:, tok], qd_lo[:, tok]),
                                    (kd_hi[:, m, :], kd_lo[:, m, :]), True, True).then_inc(dscore, 1)

                    def turn_a(n, src, ready, count):
                        pe.wait_ge(ready, count)
                        if n >= 2:
                            pe.wait_ge(at_lo, hd * (2 * TT) + (n - 1))
                        for j in range(TT):
                            last = pe.transpose(ps[:, 6 + n % 2, j * P:(j + 1) * P],
                                                src[:, j * P:(j + 1) * P], ident[:])
                        last.then_inc(at_out, 1)

                    def d_turn(t):
                        turn_a(t, prb[:, 2 * (t % 2), :], dnorm, hd * (4 * TT) + (4 * t + 4))

                    def m_turn(t):
                        turn_a(4 + t, prb[:, t, :], mnorm, hd * (2 * TT) + (2 * t + 2))

                    def pv(n, bank, v):
                        pe.wait_ge(at_lo, hd * (2 * TT) + (2 * n + 2))
                        for j in range(TT):
                            cols = slice(j * P, (j + 1) * P)
                            last = product(ps[:, bank, (n % 2) * HALF:(n % 2 + 1) * HALF],
                                           (v[0][:, cols], v[1][:, cols]),
                                           (a_hi[:, n % 2, j, :], a_lo[:, n % 2, j, :]), j == 0, j == TT - 1)
                        last.then_inc(pv_out, 1)

                    def m_scores(t):
                        tok = slice(t * P, (t + 1) * P)
                        pe.wait_ge(dbias, hd * (2 * TT) + (TT + t + 1))
                        product(ps[:, 2 + t, :], (qn_hi[:, tok], qn_lo[:, tok]), (kn_hi[:], kn_lo[:]), True, False)
                        product(ps[:, 2 + t, :], (qr_hi[:, tok], qr_lo[:, tok]), (kr_hi[:], kr_lo[:]),
                                False, True).then_inc(mscore, 1)

                    pe.wait_ge(mexp, hd * TT + BANKS)
                    pe.wait_ge(wo_added, hd * (2 * TT) + BANKS)
                    bank_split(8)
                    d_scores(0)
                    d_scores(1)
                    for t in range(TT):
                        d_turn(t)
                        if t + 2 < TT:
                            d_scores(t + 2)
                        else:
                            m_scores(t - 2)
                    pv(0, 1, (vd_hi, vd_lo))
                    pv(1, 1, (vd_hi, vd_lo))
                    m_scores(2)
                    m_scores(3)
                    m_turn(0)
                    pe.wait_ge(sq_done, hd + 1)
                    for t in range(TT):
                        last = pe.matmul(ps[:, 1, t:t + 1], sq[:, t * P:(t + 1) * P], ones[:], start=True,
                                         stop=True)
                    last.then_inc(ms_out, 1)
                    m_turn(1)
                    m_turn(2)
                    pv(2, 0, (vm_hi, vm_lo))
                    m_turn(3)
                    pe.wait_ge(rb_done, hd + 1)
                    for t in range(TT):
                        last = pe.transpose(ps[:, 1, t * P:(t + 1) * P], rb[:, t, :], ident[:])
                    last.then_inc(rbT_out, 1)
                    pv(3, 0, (vm_hi, vm_lo))
                    split_unit(rnd, 4)
                    split_unit(rnd, 5)
                    pe.wait_ge(od_lo_done, hd + 1)
                    pe.wait_ge(om_lo_done, hd + 1)
                    add_rows(rnd, hd * (2 * TT), [(od_hi, od_lo), (om_hi, om_lo)], wo_out, wo_added)
                ln_pe(lay, 1)
                ffn_pe(lay, 1, FR + 1 + HEADS)
                ln_pe(lay, 2)


_INS = ["x", "ffn1_w_gate", "ffn1_w_up", "ffn1_w_down", "ln1_g", "ln1_b", "w_in", "q_norm_g", "w_q_up",
        "kv_norm_g", "w_kv_up", "diff_lambda_q1", "diff_lambda_k1", "diff_lambda_q2", "diff_lambda_k2",
        "diff_subln_g", "w_out", "ln2_g", "ln2_b", "ffn2_w_gate", "ffn2_w_up", "ffn2_w_down", "ln3_g", "ln3_b"]


def constants():
    import math
    pos = np.arange(S, dtype=np.float32)
    inv = (np.float32(10000.0) ** (-np.arange(0, ROPE, 2, dtype=np.float32) / np.float32(ROPE))).astype(np.float32)
    ang = inv[:, None] * pos[None, :]
    c, s = np.cos(ang).astype(np.float32), np.sin(ang).astype(np.float32)
    part, col = np.arange(P)[:, None], np.arange(DIST)[None, :]
    init = [0.8 - 0.6 * math.exp(-0.3 * lay) for lay in range(DEPTH)]
    return {
        "ident": np.eye(P, dtype=np.float32),
        "dist": np.abs(part - col + (S - P)).astype(np.float32),
        "cos": np.concatenate([c, c]),
        "sin": np.concatenate([s, -s]),
        "lam": np.array([[v, 1.0 - v] for v in init], np.float32),
    }


def kernel(**inputs):
    import concourse.bacc as bacc
    from concourse.bass_utils import run_bass_kernel_spmd as run

    nc = bacc.Bacc("TRN2", target_bir_lowering=False, num_devices=1)
    arrays, args = {}, []
    for name in _INS:
        arrays[name] = np.ascontiguousarray(inputs[name])
    for name, a in constants().items():
        arrays["const_" + name] = a
    for name, a in arrays.items():
        args.append(nc.dram_tensor(name, a.shape, mybir.dt.from_np(a.dtype), kind="ExternalInput").ap())
    args.append(nc.dram_tensor("encoded", (1, S, D), F32, kind="ExternalOutput").ap())
    build(nc, *args)
    r = run(nc, [arrays], core_ids=[0])
    return r.results[0]["encoded"]
```

```python
from contextlib import ExitStack

import numpy as np
import concourse.bass as bass
from concourse import mybir

F32 = mybir.dt.float32
F32R = mybir.dt.float32r
ALU = mybir.AluOpType
ACT = mybir.ActivationFunctionType
AX = mybir.AxisListType

P = 128
D = 1024
S = 512
DEPTH = 2
F = 2816
HEADS = 4
NOPE, ROPE, VD = 128, 64, 128
QR, KVR = 256, 128
DH = 64
LAT = QR + KVR + ROPE
DQ0 = LAT
DK0 = DQ0 + HEADS * 2 * DH
DV0 = DK0 + HEADS * 2 * DH
EPS = 1e-5
ALPHA = (2 * DEPTH) ** 0.25
LN_EPS = EPS / ALPHA ** 2
KB = D // P
TT = S // P
FR = F // (2 * P)
UNITS = 6
RAW = 3
BANKS = 4
LATENT_BANK = 4
C_BANK = (6, 1, 4, 0)
PREPARED = 19
RG = (2, 2, 1, 1, 1, 1)
RG0 = (0, 2, 4, 5, 6, 7)
ROUNDS = 2 * FR + 1 + HEADS
LNS = 3
MLA_SCALE = (NOPE + ROPE) ** -0.5
DIFF_SCALE = DH ** -0.5
DIST = S + S - P
HALF = S // 2


def build(nc, x, g1, u1, d1, ln1_g, ln1_b, w_in, q_norm_g, w_q_up, kv_norm_g, w_kv_up, lq1, lk1, lq2, lk2,
          subln_g, w_out, ln2_g, ln2_b, g2, u2, d2, ln3_g, ln3_b, c_ident, c_alibi, c_cos, c_sin, c_lam, out):
    ctx = ExitStack()
    with ctx:
        def sem(name):
            return ctx.enter_context(nc.semaphore(name))

        slab_bytes = nc.sbuf_usable_end - nc.sbuf_base - 64
        base = (nc.sbuf_base + 63) // 32 * 32
        ctx.enter_context(nc.sbuf_tensor("slab", [P, slab_bytes // 4 - 8], F32))
        top = [base]

        def size(shape):
            return int(np.prod(shape[1:])) * 4

        def at(offset, name, shape, dt=F32):
            assert offset + size(shape) <= base + slab_bytes, (name, offset + size(shape) - base - slab_bytes)
            return nc.alloc_sbuf_tensor_at(name, list(shape), dt, offset=offset)

        def sb(name, shape, dt=F32):
            t = at(top[0], name, shape, dt)
            top[0] += (size(shape) + 31) // 32 * 32
            return t

        def shared(*groups):
            start, end, made = top[0], top[0], []
            for group in groups:
                top[0] = start
                made += [sb(*one) for one in group]
                end = max(end, top[0])
            top[0] = end
            return made

        x_tok = sb("x_tok", [P, TT, D])
        x_hi = sb("x_hi", [P, KB, S], F32R)
        x_lo = sb("x_lo", [P, KB, S], F32R)
        raw = sb("raw", [P, RAW, D])
        w_hi = sb("w_hi", [P, UNITS, D], F32R)
        w_lo = sb("w_lo", [P, UNITS, D], F32R)
        (qd_hi, qd_lo, vd_hi, vd_lo, qn_hi, qn_lo, kn_hi, kn_lo, vm_hi, vm_lo,
         silu, prod, h_hi, h_lo, xg) = shared(
            [(n, [P, S], F32R) for n in ("qd_hi", "qd_lo", "vd_hi", "vd_lo", "qn_hi", "qn_lo",
                                         "kn_hi", "kn_lo", "vm_hi", "vm_lo")],
            [("silu", [P, 2, S], F32), ("prod", [P, 2, S], F32),
             ("h_hi", [P, 2, S], F32R), ("h_lo", [P, 2, S], F32R)],
            [("xg", [P, KB, S], F32)])
        kd_hi = sb("kd_hi", [P, 2, S], F32R)
        kd_lo = sb("kd_lo", [P, 2, S], F32R)
        qr_hi = sb("qr_hi", [P, S], F32R)
        qr_lo = sb("qr_lo", [P, S], F32R)
        kr_hi = sb("kr_hi", [P, S], F32R)
        kr_lo = sb("kr_lo", [P, S], F32R)
        c_hi, c_lo, ln_gb = shared([("c_hi", [P, 3, S], F32R), ("c_lo", [P, 3, S], F32R)],
                                   [("ln_gb", [P, 2, D], F32)])
        prb, c_tok, junk, lam_in, lam_junk = shared(
            [("prb", [P, 4, S], F32)],
            [("c_tok", [P, TT, LAT], F32), ("junk", [P, QR + KVR], F32)],
            [("lam_in", [P, 4, DH], F32), ("lam_junk", [P, 2, DH], F32)])
        a_hi = sb("a_hi", [P, 2, TT, HALF], F32R)
        a_lo = sb("a_lo", [P, 2, TT, HALF], F32R)
        od_hi = sb("od_hi", [P, S], F32R)
        od_lo = sb("od_lo", [P, S], F32R)
        om_hi = sb("om_hi", [P, S], F32R)
        om_lo = sb("om_lo", [P, S], F32R)
        od, sq, rb, rope_s, rope_w, vt, lat_g = shared(
            [("od", [P, S], F32), ("sq", [P, S], F32), ("rb", [P, TT, P], F32)],
            [("rope_s", [P, S], F32), ("rope_w", [P, S], F32), ("vt", [P, S], F32)],
            [("lat_g", [P, QR + KVR], F32)])
        alibi = sb("alibi", [P, DIST])
        cos = sb("cos", [P, S])
        sin = sb("sin", [P, S])
        ident = sb("ident", [P, P])
        lam_k = sb("lam_k", [P, 2])
        sub_g = sb("sub_g", [P, 1])
        sub_gs = sb("sub_gs", [P, 1])
        dots = sb("dots", [P, 2])
        edots = sb("edots", [P, 2])
        nlam = sb("nlam", [P, 2])
        ones = sb("ones", [P, 1])
        mhalf = sb("mhalf", [P, 8])
        wait_seat = sb("wait_seat", [P, 1])
        minus = sb("minus", [P, 1])
        ln_eps = sb("ln_eps", [P, 1])
        eps8 = sb("eps8", [P, 8])
        lat_n = sb("lat_n", [P, 8])
        gb_t = sb("gb_t", [P, 2, KB])
        nmean = sb("nmean", [P, TT])
        stats = sb("stats", [P, TT, 12])
        mv = sb("mv", [P, TT, 2])
        ve = sb("ve", [P, TT])
        rstd = sb("rstd", [P, TT])
        nmr = sb("nmr", [P, TT])
        ss = sb("ss", [P, 8])
        ssv = sb("ssv", [P, 8])
        rc = sb("rc", [P, 8])
        dmax = sb("dmax", [P, TT, 2])
        dneg = sb("dneg", [P, TT, 2])
        dsum = sb("dsum", [P, TT, 2])
        drec = sb("drec", [P, TT, 2])
        drl = sb("drl", [P, TT])
        mmax = sb("mmax", [P, TT])
        mneg = sb("mneg", [P, TT])
        msum = sb("msum", [P, TT])
        mrec = sb("mrec", [P, TT])
        ms = sb("ms", [P, TT])
        rms = sb("rms", [P, TT])

        ps = ctx.enter_context(nc.psum_tensor("ps", [P, 8, S], F32))

        const_landed = sem("const_landed")
        ident_landed = sem("ident_landed")
        x_landed = sem("x_landed")
        param_landed = sem("param_landed")
        gb_landed = sem("gb_landed")
        landed = [sem(f"landed{s}") for s in range(UNITS)]
        kvup_landed = sem("kvup_landed")
        stored = sem("stored")
        hi_done = sem("hi_done")
        lo_done = sem("lo_done")
        used = [sem(f"used{s}") for s in range(UNITS)]
        prepared = sem("prepared")
        silu_done, prod_done = sem("silu_done"), sem("prod_done")
        h_hi_done, h_lo_done = sem("h_hi_done"), sem("h_lo_done")
        down_out, down_added = sem("down_out"), sem("down_added")
        ln_stat, ln_agg, ln_pool = sem("ln_stat"), sem("ln_agg"), sem("ln_pool")
        ln_norm, ln_scaled = sem("ln_norm"), sem("ln_scaled")
        xt_out, xt_scaled, xt_lo_done = sem("xt_out"), sem("xt_scaled"), sem("xt_lo_done")
        xt_hi_even, xt_hi_odd = sem("xt_hi_even"), sem("xt_hi_odd")
        lat_out, lat_sq, lat_pool, lat_scaled = sem("lat_out"), sem("lat_sq"), sem("lat_pool"), sem("lat_scaled")
        latT_out, latT_hi, latT_lo = sem("latT_out"), sem("latT_hi"), sem("latT_lo")
        rope_swapped, rope_cos, rope_sum = sem("rope_swapped"), sem("rope_cos"), sem("rope_sum")
        rope_hi, rope_lo = sem("rope_hi"), sem("rope_lo")
        lam_dot, lam_exp, lam_step = sem("lam_dot"), sem("lam_exp"), sem("lam_step")
        alibi_set = sem("alibi_set")
        proj_out, proj_hi, proj_lo = sem("proj_out"), sem("proj_hi"), sem("proj_lo")
        vt_copied, vt_out = sem("vt_copied"), sem("vt_out")
        dscore, dbias, dneg_done, dexp = sem("dscore"), sem("dbias"), sem("dneg_done"), sem("dexp")
        dscaled, dnorm = sem("dscaled"), sem("dnorm")
        mscore, mmax_done, mneg_done, mexp, mnorm = (sem("mscore"), sem("mmax_done"), sem("mneg_done"),
                                                     sem("mexp"), sem("mnorm"))
        at_out, at_hi, at_lo = sem("at_out"), sem("at_hi"), sem("at_lo")
        pv_out = sem("pv_out")
        od_copied, sq_done, ms_out, ms_copied, rms_done = (sem("od_copied"), sem("sq_done"), sem("ms_out"),
                                                           sem("ms_copied"), sem("rms_done"))
        rb_done, rbT_out, od_scaled, od_hi_done, od_lo_done = (sem("rb_done"), sem("rbT_out"), sem("od_scaled"),
                                                               sem("od_hi_done"), sem("od_lo_done"))
        om_hi_done, om_lo_done = sem("om_hi_done"), sem("om_lo_done")
        wo_out, wo_added = sem("wo_out"), sem("wo_added")

        def raw32(t):
            return t.bitcast(F32)

        def rows(w):
            return w.rearrange("(k p) f -> p k f", p=P)

        LAT_W = [n * LAT for n in RG]
        HEAD_W = [D, D, D, 2 * (NOPE + ROPE) + NOPE + VD, D, D]
        MQ = NOPE + ROPE

        block = ctx.enter_context(nc.Block())

        @block.sync
        def _(sp):
            def unit(rnd, s, dst_w, src, shape=None):
                sp.wait_ge(lo_done, rnd * UNITS + (s + 1))
                dst = raw[:, s % RAW, 0:dst_w]
                if shape is not None:
                    dst = dst.rearrange("p (k f) -> p k f", k=shape)
                sp.dma_start(dst, src).then_inc(landed[s], 16)

            def ffn_loads(lay, base_rnd, wg, wu, wd):
                with sp.Fori(0, FR) as i:
                    rnd = sp.snap(lay * ROUNDS + base_rnd + i)
                    for j in range(2):
                        cols = bass.ds(i * (2 * P) + j * P, P)
                        unit(rnd, 2 * j, D, rows(wg[lay])[:, :, cols], KB)
                        unit(rnd, 2 * j + 1, D, rows(wu[lay])[:, :, cols], KB)
                    for j in range(2):
                        unit(rnd, 4 + j, D, wd[lay, bass.ds(i * (2 * P) + j * P, P), :])

            def gb_load(lay, which, g, b):
                sp.wait_ge(ln_scaled, (lay * LNS + which + 1) * (2 * TT))
                sp.dma_start(ln_gb[:, 0, :], g[lay].partition_broadcast(P)).then_inc(gb_landed, 16)
                sp.dma_start(ln_gb[:, 1, :], b[lay].partition_broadcast(P)).then_inc(gb_landed, 16)
                sp.dma_start(gb_t[:, 0, :], g[lay].rearrange("(k p) -> p k", p=P),
                             allow_slow_non_contiguous=True).then_inc(gb_landed, 16)
                sp.dma_start(gb_t[:, 1, :], b[lay].rearrange("(k p) -> p k", p=P),
                             allow_slow_non_contiguous=True).then_inc(gb_landed, 16)

            for t in range(TT):
                sp.dma_start(x_tok[:, t, :], x[0, t * P:(t + 1) * P, :]).then_inc(x_landed, 16)
            sp.dma_start(ident[:], c_ident).then_inc(ident_landed, 16)
            sp.dma_start(alibi[:], c_alibi).then_inc(const_landed, 16)
            sp.dma_start(cos[P // 2:, :], c_cos).then_inc(const_landed, 16)
            sp.dma_start(sin[P // 2:, :], c_sin).then_inc(const_landed, 16)
            with sp.Fori(0, DEPTH) as lay:
                sp.wait_ge(wo_added, lay * (HEADS * 2 * TT) + BANKS)
                sp.dma_start(lat_g[:, 0:QR], q_norm_g[lay].partition_broadcast(P)).then_inc(param_landed, 16)
                sp.dma_start(lat_g[:, QR:], kv_norm_g[lay].partition_broadcast(P)).then_inc(param_landed, 16)
                for n, v in enumerate((lq1, lk1, lq2, lk2)):
                    sp.dma_start(lam_in[:, n, :], v[lay].partition_broadcast(P)).then_inc(param_landed, 16)
                sp.dma_start(lam_k[:], c_lam[lay].partition_broadcast(P)).then_inc(param_landed, 16)
                sp.dma_start(sub_g[:], subln_g[lay].rearrange("(p a) -> p a", a=1)).then_inc(param_landed, 16)
                ffn_loads(lay, 0, g1, u1, d1)
                gb_load(lay, 0, ln1_g, ln1_b)
                rnd = sp.snap(lay * ROUNDS + FR)
                for s in range(UNITS):
                    src = rows(w_in[lay])[:, RG0[s]:RG0[s] + RG[s], 0:LAT]
                    unit(rnd, s, LAT_W[s], src, RG[s])
                with sp.Fori(0, HEADS) as h:
                    rnd = sp.snap(lay * ROUNDS + (FR + 1) + h)
                    for s, c0 in enumerate((DQ0, DK0, DV0)):
                        unit(rnd, s, D, rows(w_in[lay])[:, :, bass.ds(h * P + c0, P)], KB)
                    unit(rnd, 3, 2 * MQ, rows(w_q_up[lay])[:, :, bass.ds(h * MQ, MQ)], 2)
                    sp.dma_start(raw[:, 0, 2 * MQ:2 * MQ + NOPE + VD],
                                 w_kv_up[lay, :, bass.ds(h * (NOPE + VD), NOPE + VD)]).then_inc(kvup_landed, 16)
                    unit(rnd, 4, D, w_out[lay, bass.ds(h * P + HEADS * VD, P), :])
                    unit(rnd, 5, D, w_out[lay, bass.ds(h * P, P), :])
                sp.wait_ge(proj_lo, (lay * HEADS + HEADS) * 7)
                gb_load(lay, 1, ln2_g, ln2_b)
                ffn_loads(lay, FR + 1 + HEADS, g2, u2, d2)
                gb_load(lay, 2, ln3_g, ln3_b)
            for t in range(TT):
                sp.wait_ge(ln_scaled, DEPTH * LNS * 2 * TT + 2 * t + 2)
                sp.dma_start(out[0, t * P:(t + 1) * P, :], x_tok[:, t, :]).then_inc(stored, 16)
            sp.wait_ge(stored, 16 * TT)

        @block.gpsimd
        def _(pool):
            pool.memset(ones[:], 1.0).then_inc(prepared, 1)
            pool.memset(mhalf[:], -0.5).then_inc(prepared, 1)
            pool.memset(minus[:], -1.0).then_inc(prepared, 1)
            pool.memset(ln_eps[:], LN_EPS).then_inc(prepared, 1)
            pool.memset(eps8[:], EPS).then_inc(prepared, 1)
            pool.memset(lat_n[:, 0:TT], 1.0 / QR).then_inc(prepared, 1)
            pool.memset(lat_n[:, TT:], 1.0 / KVR).then_inc(prepared, 1)
            for z in (ln_gb, gb_t):
                pool.memset(z[:, 0, :], 1.0).then_inc(prepared, 1)
                pool.memset(z[:, 1, :], 0.0).then_inc(prepared, 1)
            pool.sem_inc(gb_landed, 64)
            pool.sem_inc(lo_done, RAW)

            def lo_part(rnd, s, width):
                pool.wait_ge(hi_done, rnd * UNITS + (s + 1))
                pool.tensor_tensor(w_lo[:, s, 0:width], raw[:, s % RAW, 0:width], raw32(w_hi[:, s, 0:width]),
                                   ALU.subtract).then_inc(lo_done, 1)

            def ahead(rnd, widths):
                lo_part(rnd, 4, D)
                lo_part(rnd, 5, D)
                if widths is not None:
                    for s in range(4):
                        lo_part(rnd + 1, s, widths[s])

            def ffn_split(lay, base_rnd, after):
                with pool.Fori(0, FR - 1) as i:
                    ahead(pool.snap(lay * ROUNDS + base_rnd + i), [D] * 4)
                ahead(pool.snap(lay * ROUNDS + (base_rnd + FR - 1)), after)

            def ln_power(lay, w):
                ln = pool.snap(lay * LNS + w)
                for t in range(TT):
                    c = slice(t, t + 1)
                    pool.wait_ge(ln_agg, ln * TT + (t + 1))
                    pool.tensor_tensor(ve[:, c], mv[:, t, 1:2], ln_eps[:], ALU.add).then_inc(ln_pool, 1)
                    pool.tensor_tensor(nmean[:, c], mv[:, t, 0:1], minus[:], ALU.mult).then_inc(ln_pool, 1)
                    pool.wait_ge(ln_pool, ln * (4 * TT) + (4 * t + 2))
                    pool.tensor_tensor(rstd[:, c], ve[:, c], mhalf[:, 0:1], ALU.pow).then_inc(ln_pool, 1)
                    pool.wait_ge(ln_pool, ln * (4 * TT) + (4 * t + 3))
                    pool.tensor_tensor(nmr[:, c], nmean[:, c], rstd[:, c], ALU.mult).then_inc(ln_pool, 1)

            def rope(index, hi, lo):
                both = slice(P // 2, P)
                pool.wait_ge(rope_swapped, index * 2 + 2)
                pool.tensor_tensor(rope_s[both, :], rope_s[both, :], sin[both, :], ALU.mult).then_inc(rope_sum, 1)
                pool.wait_ge(rope_sum, index * 2 + 1)
                pool.wait_ge(rope_cos, index + 1)
                pool.tensor_tensor(hi[both, :], rope_w[both, :], rope_s[both, :], ALU.add).then_inc(rope_hi, 1)
                pool.tensor_tensor(rope_w[both, :], rope_w[both, :], rope_s[both, :], ALU.add)\
                    .then_inc(rope_sum, 1)
                pool.wait_ge(rope_hi, index + 1)
                pool.wait_ge(rope_sum, index * 2 + 2)
                pool.tensor_tensor(lo[both, :], rope_w[both, :], raw32(hi[both, :]), ALU.subtract)\
                    .then_inc(rope_lo, 1)

            pool.wait_ge(const_landed, 48)
            with pool.Fori(0, DEPTH) as lay:
                rnd = pool.snap(lay * ROUNDS)
                for s in range(4):
                    lo_part(rnd, s, D)
                ffn_split(lay, 0, LAT_W)
                ln_power(lay, 0)
                rnd = pool.snap(lay * ROUNDS + FR)
                for s in (4, 5):
                    lo_part(rnd, s, LAT_W[s])
                for s in range(4):
                    lo_part(rnd + 1, s, HEAD_W[s])
                pool.wait_ge(lat_sq, (lay + 1) * (2 * TT))
                pool.tensor_tensor(ssv[:], ss[:], lat_n[:], ALU.mult).then_inc(lat_pool, 1)
                pool.wait_ge(lat_pool, lay * 3 + 1)
                pool.tensor_tensor(ssv[:], ssv[:], eps8[:], ALU.add).then_inc(lat_pool, 1)
                pool.wait_ge(lat_pool, lay * 3 + 2)
                pool.tensor_tensor(rc[:], ssv[:], mhalf[:], ALU.pow).then_inc(lat_pool, 1)
                rope(lay * (HEADS + 1), kr_hi, kr_lo)

                def head(h, widths):
                    rnd = pool.snap(h + (lay * ROUNDS + (FR + 1)))
                    rope(pool.snap(h + (lay * (HEADS + 1) + 1)), qr_hi, qr_lo)
                    lo_part(rnd, 4, D)
                    lo_part(rnd, 5, D)
                    pool.wait_ge(ms_copied, lay * HEADS + h + 1)
                    pool.tensor_tensor(rms[:], ms[:], mhalf[:, 0:TT], ALU.pow).then_inc(rms_done, 1)
                    for s in range(4):
                        lo_part(rnd + 1, s, widths[s])

                with pool.Fori(0, HEADS - 1) as h:
                    head(h, HEAD_W)
                head(HEADS - 1, [D] * 4)
                ln_power(lay, 1)
                ffn_split(lay, FR + 1 + HEADS, None)
                ln_power(lay, 2)

        @block.scalar
        def _(act):
            def hi_part(rnd, s, width, also=None):
                act.wait_ge(landed[s], rnd * 16 + 16)
                if also is not None:
                    act.wait_ge(*also)
                act.wait_ge(used[s], rnd + 1)
                act.copy(w_hi[:, s, 0:width], raw[:, s % RAW, 0:width]).then_inc(hi_done, 1)

            def ffn_act(lay, which, base_rnd, after):
                def one(i, widths):
                    rnd = act.snap(i + (lay * ROUNDS + base_rnd))
                    ffn = act.snap(i + (lay * (2 * FR) + which * FR))

                    def silu_of(j):
                        act.wait_ge(used[2 * j], rnd + 2)
                        act.activation(silu[:, j, :], ps[:, 2 * j, :], ACT.Silu).then_inc(silu_done, 1)

                    def h_part(j):
                        act.wait_ge(prod_done, ffn * 2 + (j + 1))
                        act.wait_ge(used[5], rnd + 1)
                        act.copy(h_hi[:, j, :], prod[:, j, :]).then_inc(h_hi_done, 1)

                    def next_part(s):
                        if widths is not None:
                            hi_part(rnd + 1, s, widths[s])

                    hi_part(rnd, 4, D)
                    hi_part(rnd, 5, D)
                    next_part(0)
                    silu_of(0)
                    h_part(0)
                    next_part(1)
                    silu_of(1)
                    next_part(2)
                    h_part(1)
                    next_part(3)

                with act.Fori(0, FR - 1) as i:
                    one(i, [D] * 4)
                one(FR - 1, after)

            def norm(lay, which):
                ln = act.snap(lay * LNS + which)
                for t in range(TT):
                    act.wait_ge(ln_pool, ln * (4 * TT) + (4 * t + 4))
                    act.activation(x_tok[:, t, :], x_tok[:, t, :], ACT.Identity, bias=nmr[:, t:t + 1],
                                   scale=rstd[:, t:t + 1]).then_inc(ln_norm, 1)

            def turned(epoch, shift):
                act.wait_ge(gb_landed, epoch * 64 + 64)
                for k in range(KB):
                    act.wait_ge(xt_out, epoch * KB + (k + 1))
                    act.activation(xg[:, k, :], ps[:, (k + shift) % KB, :], ACT.Identity,
                                   bias=gb_t[:, 1, k:k + 1], scale=gb_t[:, 0, k:k + 1]).then_inc(xt_scaled, 1)
                    if k % 2 == 0:
                        act.wait_ge(xt_scaled, epoch * KB + (k + 1))
                        act.copy(x_hi[:, k, :], xg[:, k, :]).then_inc(xt_hi_even, 1)

            def swap_halves(index, bank):
                a, b = slice(P // 2, P // 2 + ROPE // 2), slice(P // 2 + ROPE // 2, P)
                act.wait_ge(rope_cos, index + 1)
                act.copy(rope_s[a, :], ps[b, bank, :]).then_inc(rope_swapped, 1)
                act.copy(rope_s[b, :], ps[a, bank, :]).then_inc(rope_swapped, 1)

            def head_unit(rnd, s, hd):
                hi_part(rnd, s, HEAD_W[s], also=(kvup_landed, hd * 16 + 16) if s == 3 else None)

            def head_units(rnd, hd):
                for s in range(4):
                    head_unit(rnd, s, hd)

            act.sem_inc(mexp, BANKS)
            act.wait_ge(prepared, PREPARED)
            act.wait_ge(x_landed, 16 * TT)
            act.sem_inc(ln_norm, TT)
            with act.Fori(0, DEPTH) as lay:
                act.wait_ge(lam_dot, lay * 2 + 2)
                act.activation(edots[:], dots[:], ACT.Exp).then_inc(lam_exp, 1)
                rnd = act.snap(lay * ROUNDS)
                hi_part(rnd, 0, D)
                hi_part(rnd, 1, D)
                turned(act.snap(lay * LNS), 0)
                hi_part(rnd, 2, D)
                hi_part(rnd, 3, D)
                ffn_act(lay, 0, 0, LAT_W)
                norm(lay, 0)
                turned(act.snap(lay * LNS + 1), LATENT_BANK)
                rnd = act.snap(lay * ROUNDS + FR)
                for s in (4, 5):
                    hi_part(rnd, s, LAT_W[s])
                head_units(rnd + 1, lay * HEADS)
                for t in range(TT):
                    if t < TT - 1:
                        act.wait_ge(lat_out, lay * (TT - 1) + (t + 1))
                    else:
                        act.wait_ge(used[5], rnd + 2)
                    if t > 0:
                        act.wait_ge(lat_sq, lay * (2 * TT) + 2 * t)
                    act.activation(junk[:, 0:QR], ps[:, LATENT_BANK + t, 0:QR], ACT.Square,
                                   accum_out=ss[:, t:t + 1]).then_inc(lat_sq, 1)
                    act.activation(junk[:, QR:], ps[:, LATENT_BANK + t, QR:QR + KVR], ACT.Square,
                                   accum_out=ss[:, TT + t:TT + t + 1]).then_inc(lat_sq, 1)
                act.wait_ge(ln_scaled, (lay * LNS + 2) * (2 * TT))
                for f in range(3):
                    act.wait_ge(latT_out, lay * 4 + (f + 1))
                    act.copy(c_hi[:, f, :], ps[:, C_BANK[f], :]).then_inc(latT_hi, 1)
                swap_halves(lay * (HEADS + 1), C_BANK[3])
                def head(h, more):
                    rnd = act.snap(h + (lay * ROUNDS + (FR + 1)))
                    hd = act.snap(h + lay * HEADS)

                    def unit_product(s):
                        act.wait_ge(used[s], rnd + 2)

                    def proj(dst, src):
                        act.copy(dst, src).then_inc(proj_hi, 1)

                    def next_part(s):
                        if more:
                            head_unit(rnd + 1, s, hd + 1)
                        else:
                            hi_part(rnd + 1, s, D)

                    def a_part(n):
                        act.wait_ge(at_out, hd * (2 * TT) + (n + 1))
                        if n % 2 == 0:
                            act.wait_ge(pv_out, hd * 4 + (n // 2 + 1))
                        act.copy(a_hi[:, n // 2 % 2, :, (n % 2) * P:(n % 2 + 1) * P],
                                 ps[:, 6 + n % 2, :].rearrange("p (j q) -> p j q", j=TT)).then_inc(at_hi, 1)

                    def d_exp(t):
                        act.wait_ge(dneg_done, hd * TT + (t + 1))
                        for m in range(2):
                            p = prb[:, 2 * (t % 2) + m, :]
                            act.activation(p, p, ACT.Exp, bias=dneg[:, t, m:m + 1],
                                           accum_out=dsum[:, t, m:m + 1]).then_inc(dexp, 1)

                    def d_scale(t):
                        act.wait_ge(dnorm, hd * (3 * TT) + (3 * t + 1))
                        p1 = prb[:, 2 * (t % 2), :]
                        act.activation(p1, p1, ACT.Copy, scale=drec[:, t, 0:1]).then_inc(dscaled, 1)

                    def m_exp(t):
                        act.wait_ge(mneg_done, hd * TT + (t + 1))
                        act.wait_ge(at_out, hd * (2 * TT) + (3 + t // 2))
                        act.activation(prb[:, t, :], ps[:, 2 + t, :], ACT.Exp, bias=mneg[:, t:t + 1],
                                       scale=MLA_SCALE, accum_out=msum[:, t:t + 1]).then_inc(mexp, 1)

                    unit_product(0)
                    proj(qd_hi[:], ps[:, 2, :])
                    unit_product(1)
                    for m in range(2):
                        half = slice(m * DH, (m + 1) * DH)
                        proj(kd_hi[half, m, :], ps[half, 3, :])
                    unit_product(2)
                    act.copy(vt[:], ps[:, 7, :]).then_inc(vt_copied, 1)
                    d_exp(0)
                    swap_halves(h + (lay * (HEADS + 1) + 1), 0)
                    d_scale(0)
                    d_exp(1)
                    act.wait_ge(vt_out, hd + 1)
                    proj(vd_hi[:], ps[:, 6, :])
                    act.wait_ge(proj_out, hd * 3 + 2)
                    proj(qn_hi[:], ps[:, 1, :])
                    d_scale(1)
                    act.wait_ge(proj_out, hd * 3 + 3)
                    proj(kn_hi[:], ps[:, 7, :])
                    unit_product(3)
                    proj(vm_hi[:], ps[:, 2, :])
                    a_part(0)
                    d_exp(2)
                    a_part(1)
                    d_scale(2)
                    d_exp(3)
                    a_part(2)
                    d_scale(3)
                    m_exp(0)
                    a_part(3)
                    m_exp(1)
                    m_exp(2)
                    m_exp(3)
                    hi_part(rnd, 4, D)
                    a_part(4)
                    act.wait_ge(pv_out, hd * 4 + (2 + 2))
                    act.activation(sq[:], ps[:, 0, :], ACT.Square).then_inc(sq_done, 1)
                    act.copy(od[:], ps[:, 0, :]).then_inc(od_copied, 1)
                    a_part(5)
                    hi_part(rnd, 5, D)
                    a_part(6)
                    a_part(7)
                    next_part(0)
                    act.wait_ge(pv_out, hd * 4 + (2 + 4))
                    act.copy(om_hi[:], ps[:, 4, :]).then_inc(om_hi_done, 1)
                    next_part(1)
                    act.wait_ge(od_scaled, hd + 1)
                    act.copy(od_hi[:], od[:]).then_inc(od_hi_done, 1)
                    next_part(2)
                    next_part(3)

                with act.Fori(0, HEADS - 1) as h:
                    head(h, True)
                head(HEADS - 1, False)
                norm(lay, 1)
                turned(act.snap(lay * LNS + 2), 0)
                ffn_act(lay, 1, FR + 1 + HEADS, None)
                norm(lay, 2)

        @block.vector
        def _(dve):
            def rest(lo, src, hi):
                return dve.tensor_tensor(lo, src, raw32(hi), ALU.subtract)

            def stat(ln, t, added, count):
                dve.wait_ge(added, count)
                for b in range(2):
                    dve.bn_stats(stats[:, t, 6 * b:6 * b + 6], x_tok[:, t, b * S:(b + 1) * S])\
                        .then_inc(ln_stat, 1)
                dve.wait_ge(ln_stat, ln * (2 * TT) + (2 * t + 2))
                dve.memset(wait_seat[:], 0.0)
                dve.bn_aggr(mv[:, t, :], stats[:, t, :]).then_inc(ln_agg, 1)

            def add_and_stat(ln, add, added, count):
                for b in range(2 * TT):
                    add(b)
                    if b >= 2 and b % 2 == 0:
                        stat(ln, b // 2 - 1, added, count + b)
                stat(ln, TT - 1, added, count + 2 * TT)

            def turned_lo(epoch):
                for k in range(KB):
                    dve.wait_ge(xt_scaled, epoch * KB + (k + 1))
                    if k % 2 == 0:
                        dve.wait_ge(xt_hi_even, epoch * (KB // 2) + (k // 2 + 1))
                    else:
                        dve.tensor_copy(x_hi[:, k, :], xg[:, k, :]).then_inc(xt_hi_odd, 1)
                        dve.wait_ge(xt_hi_odd, epoch * (KB // 2) + (k // 2 + 1))
                    rest(x_lo[:, k, :], xg[:, k, :], x_hi[:, k, :]).then_inc(xt_lo_done, 1)

            def gains(epoch):
                dve.wait_ge(gb_landed, epoch * 64 + 64)
                for t in range(TT):
                    dve.wait_ge(ln_norm, epoch * TT + (t + 1))
                    xs = x_tok[:, t, :]
                    dve.tensor_tensor(xs, xs, ln_gb[:, 0, :], ALU.mult).then_inc(ln_scaled, 1)
                    dve.wait_ge(ln_scaled, epoch * (2 * TT) + (2 * t + 1))
                    dve.tensor_tensor(xs, xs, ln_gb[:, 1, :], ALU.add).then_inc(ln_scaled, 1)

            def ffn_dve(lay, which):
                def one(i, last):
                    rnd = dve.snap(i + (lay * ROUNDS + (which * (FR + 1 + HEADS))))
                    ffn = dve.snap(i + (lay * (2 * FR) + which * FR))
                    for j in range(2):
                        dve.wait_ge(silu_done, ffn * 2 + (j + 1))
                        dve.wait_ge(used[2 * j + 1], rnd + 2)
                        dve.tensor_tensor(prod[:, j, :], ps[:, 2 * j + 1, :], silu[:, j, :], ALU.mult)\
                            .then_inc(prod_done, 1)
                        dve.wait_ge(h_hi_done, ffn * 2 + (j + 1))
                        rest(h_lo[:, j, :], prod[:, j, :], h_hi[:, j, :]).then_inc(h_lo_done, 1)

                    def add(b):
                        if b == 0:
                            dve.wait_ge(down_added, ffn * (2 * TT) + BANKS)
                            dve.wait_ge(ln_scaled, (lay * LNS + (2 * which + 1)) * (2 * TT))
                        xs = x_tok[:, b // 2, (b % 2) * S:(b % 2 + 1) * S]
                        if b < 2 * TT - 1:
                            dve.wait_ge(down_out, ffn * (2 * TT - 1) + (b + 1))
                        else:
                            dve.wait_ge(used[5], rnd + 2)
                        dve.scalar_tensor_tensor(xs, ps[:, 4 + b % 4, :], 0.5 / ALPHA, xs, ALU.mult, ALU.add)\
                            .then_inc(down_added, 1)

                    if last:
                        add_and_stat(dve.snap(lay * LNS + 2 * which), add, down_added, ffn * (2 * TT) + BANKS)
                    else:
                        for b in range(2 * TT):
                            add(b)

                with dve.Fori(0, FR - 1) as i:
                    one(i, False)
                one(FR - 1, True)

            def rope(bank):
                both = slice(P // 2, P)
                dve.tensor_tensor(rope_w[both, :], ps[both, bank, :], cos[both, :], ALU.mult)\
                    .then_inc(rope_cos, 1)

            dve.sem_inc(down_added, BANKS)
            dve.sem_inc(wo_added, BANKS)
            dve.sem_inc(od_lo_done, 1)
            dve.sem_inc(om_lo_done, 1)
            for z in (kd_hi, kd_lo):
                dve.memset(raw32(z[P // 2:P, 0, :]), 0.0).then_inc(prepared, 1)
                dve.memset(raw32(z[0:P // 2, 1, :]), 0.0).then_inc(prepared, 1)
            for z in (qr_hi, qr_lo, kr_hi, kr_lo):
                dve.memset(raw32(z[0:P // 2, :]), 0.0).then_inc(prepared, 1)
            dve.wait_ge(const_landed, 48)
            dve.wait_ge(prepared, PREPARED)
            with dve.Fori(0, DEPTH) as lay:
                dve.wait_ge(param_landed, lay * 128 + 128)
                for n in range(2):
                    dve.tensor_tensor_reduce(lam_junk[:, n, :], lam_in[:, 2 * n, :], lam_in[:, 2 * n + 1, :], 1.0, 0.0,
                                             ALU.mult, ALU.add, dots[:, n:n + 1]).then_inc(lam_dot, 1)
                dve.tensor_tensor(sub_gs[:], sub_g[:], lam_k[:, 1:2], ALU.mult).then_inc(lam_step, 1)
                dve.wait_ge(lam_exp, lay + 1)
                dve.tensor_tensor(nlam[:, 0:1], edots[:, 1:2], edots[:, 0:1], ALU.subtract).then_inc(lam_step, 1)
                dve.wait_ge(lam_step, lay * 3 + 2)
                dve.tensor_tensor(nlam[:, 1:2], nlam[:, 0:1], lam_k[:, 0:1], ALU.subtract).then_inc(lam_step, 1)
                turned_lo(dve.snap(lay * LNS))
                gains(dve.snap(lay * LNS))
                ffn_dve(lay, 0)
                turned_lo(dve.snap(lay * LNS + 1))
                gains(dve.snap(lay * LNS + 1))
                dve.wait_ge(lat_pool, lay * 3 + 3)
                for t in range(TT):
                    dve.scalar_tensor_tensor(c_tok[:, t, 0:QR], ps[:, LATENT_BANK + t, 0:QR], rc[:, t:t + 1], lat_g[:, 0:QR],
                                             ALU.mult, ALU.mult).then_inc(lat_scaled, 1)
                    dve.scalar_tensor_tensor(c_tok[:, t, QR:QR + KVR], ps[:, LATENT_BANK + t, QR:QR + KVR],
                                             rc[:, TT + t:TT + t + 1], lat_g[:, QR:], ALU.mult, ALU.mult)\
                        .then_inc(lat_scaled, 1)
                    dve.tensor_copy(c_tok[:, t, QR + KVR:], ps[:, LATENT_BANK + t, QR + KVR:LAT]).then_inc(lat_scaled, 1)
                for f in range(3):
                    dve.wait_ge(latT_hi, lay * 3 + (f + 1))
                    rest(c_lo[:, f, :], ps[:, C_BANK[f], :], c_hi[:, f, :]).then_inc(latT_lo, 1)
                dve.wait_ge(latT_out, lay * 4 + 4)
                rope(C_BANK[3])
                dve.tensor_scalar(alibi[:], alibi[:], 4.0 ** HEADS, None, ALU.mult).then_inc(alibi_set, 1)
                def add_out(hd, rnd, b):
                    if b == 0:
                        dve.wait_ge(wo_added, hd * (2 * TT) + BANKS)
                        dve.wait_ge(ln_scaled, (lay * LNS + 2) * (2 * TT))
                    xs = x_tok[:, b // 2, (b % 2) * S:(b % 2 + 1) * S]
                    if b < 2 * TT - 1:
                        dve.wait_ge(wo_out, hd * (2 * TT - 1) + (b + 1))
                    else:
                        dve.wait_ge(used[5], rnd + 2)
                    dve.scalar_tensor_tensor(xs, ps[:, b % 2, :], 1.0 / ALPHA, xs, ALU.mult, ALU.add)\
                        .then_inc(wo_added, 1)

                def head(h, more):
                    rnd = dve.snap(h + (lay * ROUNDS + (FR + 1)))
                    hd = dve.snap(h + lay * HEADS)

                    def outs(*bs):
                        for b in bs:
                            if more:
                                add_out(hd - 1, rnd - 1, b)

                    def proj(n_hi, lo, src, hi):
                        dve.wait_ge(proj_hi, hd * 7 + n_hi)
                        rest(lo, src, hi).then_inc(proj_lo, 1)

                    def d_bias(t):
                        if t >= 2:
                            dve.wait_ge(at_out, hd * (2 * TT) + (t - 1))
                        if t == 0:
                            dve.wait_ge(alibi_set, h + (lay * (HEADS + 1) + 2))
                        dve.wait_ge(dscore, hd * (2 * TT) + (2 * t + 2))
                        dve.memset(wait_seat[:], 0.0)
                        for m in range(2):
                            off = (TT - 1 - t) * P
                            dve.tensor_tensor_reduce(prb[:, 2 * (t % 2) + m, :], ps[:, 2 + (2 * t + m) % 4, :],
                                                     alibi[:, off:off + S], DIFF_SCALE, -3.0e38, ALU.add, ALU.max,
                                                     dmax[:, t, m:m + 1]).then_inc(dbias, 1)
                        dve.wait_ge(dbias, hd * (2 * TT) + (2 * t + 2))
                        dve.tensor_scalar(dneg[:, t, :], dmax[:, t, :], -1.0, None, ALU.mult)\
                            .then_inc(dneg_done, 1)

                    def d_recs(t):
                        dve.wait_ge(dexp, hd * (2 * TT) + (2 * t + 2))
                        dve.reciprocal(drec[:, t, :], dsum[:, t, :]).then_inc(dnorm, 1)
                        dve.wait_ge(dnorm, hd * (3 * TT) + (3 * t + 1))
                        dve.tensor_scalar(drl[:, t:t + 1], drec[:, t, 1:2], nlam[:, 1:2], None, ALU.mult)\
                            .then_inc(dnorm, 1)

                    def d_norm(t):
                        p1, p2 = prb[:, 2 * (t % 2), :], prb[:, 2 * (t % 2) + 1, :]
                        dve.wait_ge(dscaled, hd * TT + (t + 1))
                        dve.wait_ge(dnorm, hd * (3 * TT) + (3 * t + 2))
                        dve.scalar_tensor_tensor(p1, p2, drl[:, t:t + 1], p1, ALU.mult, ALU.add)\
                            .then_inc(dnorm, 1)

                    def a_rest(n):
                        dve.wait_ge(at_hi, hd * (2 * TT) + (n + 1))
                        q = slice((n % 2) * P, (n % 2 + 1) * P)
                        rest(a_lo[:, n // 2 % 2, :, q], ps[:, 6 + n % 2, :].rearrange("p (j q) -> p j q", j=TT),
                             a_hi[:, n // 2 % 2, :, q]).then_inc(at_lo, 1)

                    def m_max(t):
                        dve.wait_ge(mscore, hd * TT + (t + 1))
                        dve.tensor_reduce(mmax[:, t:t + 1], ps[:, 2 + t, :], AX.X, ALU.max)\
                            .then_inc(mmax_done, 1)
                        dve.wait_ge(mmax_done, hd * TT + (t + 1))
                        dve.tensor_scalar(mneg[:, t:t + 1], mmax[:, t:t + 1], -MLA_SCALE, None, ALU.mult)\
                            .then_inc(mneg_done, 1)

                    def m_norm(t):
                        dve.wait_ge(mexp, hd * TT + (BANKS + t + 1))
                        dve.reciprocal(mrec[:, t:t + 1], msum[:, t:t + 1]).then_inc(mnorm, 1)
                        dve.wait_ge(mnorm, hd * (2 * TT) + (2 * t + 1))
                        dve.tensor_scalar(prb[:, t, :], prb[:, t, :], mrec[:, t:t + 1], None, ALU.mult)\
                            .then_inc(mnorm, 1)

                    dve.wait_ge(alibi_set, h + (lay * (HEADS + 1) + 1))
                    dve.tensor_scalar(alibi[:], alibi[:], 0.25, None, ALU.mult).then_inc(alibi_set, 1)
                    proj(1, qd_lo[:], ps[:, 2, :], qd_hi[:])
                    for m in range(2):
                        half = slice(m * DH, (m + 1) * DH)
                        proj(2 + m, kd_lo[half, m, :], ps[half, 3, :], kd_hi[half, m, :])
                    d_bias(0)
                    dve.wait_ge(proj_out, hd * 3 + 1)
                    rope(0)
                    d_bias(1)
                    d_recs(0)
                    d_norm(0)
                    proj(4, vd_lo[:], ps[:, 6, :], vd_hi[:])
                    d_recs(1)
                    proj(5, qn_lo[:], ps[:, 1, :], qn_hi[:])
                    outs(0)
                    d_norm(1)
                    proj(6, kn_lo[:], ps[:, 7, :], kn_hi[:])
                    proj(7, vm_lo[:], ps[:, 2, :], vm_hi[:])
                    a_rest(0)
                    d_bias(2)
                    outs(1)
                    d_recs(2)
                    d_bias(3)
                    a_rest(1)
                    outs(2)
                    d_norm(2)
                    outs(3)
                    d_recs(3)
                    outs(4)
                    d_norm(3)
                    a_rest(2)
                    m_max(0)
                    outs(5)
                    a_rest(3)
                    m_max(1)
                    m_max(2)
                    outs(6)
                    m_norm(0)
                    outs(7)
                    m_norm(1)
                    m_max(3)
                    m_norm(2)
                    a_rest(4)
                    a_rest(5)
                    m_norm(3)
                    dve.wait_ge(ms_out, hd + 1)
                    dve.tensor_scalar(ms[:], ps[:, 0, 0:TT], 1.0 / (2 * DH), EPS, ALU.mult, ALU.add)\
                        .then_inc(ms_copied, 1)
                    a_rest(6)
                    a_rest(7)
                    dve.wait_ge(rms_done, hd + 1)
                    dve.tensor_copy(rb[:], rms[:].rearrange("p (t a) -> p t a", a=1).to_broadcast([P, TT, P]))\
                        .then_inc(rb_done, 1)
                    dve.wait_ge(om_hi_done, hd + 1)
                    rest(om_lo[:], ps[:, 4, :], om_hi[:]).then_inc(om_lo_done, 1)
                    dve.wait_ge(rbT_out, hd + 1)
                    dve.scalar_tensor_tensor(od[:], ps[:, 0, :], sub_gs[:], od[:], ALU.mult, ALU.mult)\
                        .then_inc(od_scaled, 1)
                    dve.wait_ge(od_hi_done, hd + 1)
                    rest(od_lo[:], od[:], od_hi[:]).then_inc(od_lo_done, 1)

                head(0, False)
                with dve.Fori(1, HEADS) as h:
                    head(h, True)
                rnd = dve.snap(lay * ROUNDS + (FR + HEADS))
                hd = dve.snap(lay * HEADS + (HEADS - 1))
                add_and_stat(dve.snap(lay * LNS + 1), lambda b: add_out(hd, rnd, b), wo_added,
                             hd * (2 * TT) + BANKS)
                turned_lo(dve.snap(lay * LNS + 2))
                gains(dve.snap(lay * LNS + 2))
                ffn_dve(lay, 1)
            gains(DEPTH * LNS)

        @block.tensor
        def _(pe):
            for s in range(UNITS):
                pe.sem_inc(used[s], 1)
            pe.sem_inc(pv_out, 2)

            def product(out, left, right, first, last):
                pe.matmul(out, left[0], right[0], start=first, stop=False)
                pe.matmul(out, left[0], right[1], start=False, stop=False)
                return pe.matmul(out, left[1], right[0], start=False, stop=last)

            def split_unit(rnd, s):
                pe.wait_ge(lo_done, rnd * UNITS + (RAW + s + 1))

            def w(s, cols):
                return w_hi[:, s, cols], w_lo[:, s, cols]

            def xt(k, q=slice(0, S)):
                return x_hi[:, k, q], x_lo[:, k, q]

            def turn_x(epoch, shift, late_banks, added, count):
                def turn(t, k):
                    return pe.transpose(ps[:, (k + shift) % KB, t * P:(t + 1) * P],
                                        x_tok[:, t, k * P:(k + 1) * P], ident[:])

                late = [k for k in range(KB) if (k + shift) % KB in late_banks]
                for t in range(TT - 1):
                    pe.wait_ge(ln_norm, epoch * TT + (t + 1))
                    for k in range(KB):
                        if k not in late:
                            turn(t, k)
                pe.wait_ge(added, count)
                for t in range(TT - 1):
                    for k in late:
                        turn(t, k)
                pe.wait_ge(ln_norm, epoch * TT + TT)
                for k in range(KB):
                    turn(TT - 1, k).then_inc(xt_out, 1)

            def add_rows(rnd, base_index, lefts, out_sem, added_sem):
                for b in range(2 * TT):
                    t, half = b // 2, slice((b % 2) * S, (b % 2 + 1) * S)
                    pe.wait_ge(added_sem, base_index + (b + 1))
                    tok = slice(t * P, (t + 1) * P)
                    for j in range(2):
                        hi, lo = lefts[j]
                        last = product(ps[:, 4 + b % 4, :], (hi[:, tok], lo[:, tok]), w(4 + j, half),
                                       j == 0, j == 1)
                        if b == 2 * TT - 1:
                            last.then_inc(used[4 + j], 1)
                        elif j == 1:
                            last.then_inc(out_sem, 1)

            def ffn_pe(lay, which, base_rnd):
                def unit(rnd, s, epoch=None):
                    split_unit(rnd, s)
                    for k in range(KB):
                        if epoch is not None:
                            pe.wait_ge(xt_lo_done, epoch * KB + (k + 1))
                        last = product(ps[:, s, :], w(s, slice(k * P, (k + 1) * P)), xt(k),
                                       k == 0, k == KB - 1)
                    last.then_inc(used[s], 1)

                def one(i, more):
                    rnd = pe.snap(i + (lay * ROUNDS + base_rnd))
                    ffn = pe.snap(i + (lay * (2 * FR) + which * FR))
                    for s in range(1, 4):
                        unit(rnd, s)
                    if more:
                        pe.wait_ge(silu_done, ffn * 2 + 1)
                        unit(rnd + 1, 0)
                    split_unit(rnd, 4)
                    split_unit(rnd, 5)
                    pe.wait_ge(h_lo_done, ffn * 2 + 2)
                    add_rows(rnd, ffn * (2 * TT), [(h_hi[:, j, :], h_lo[:, j, :]) for j in range(2)],
                             down_out, down_added)

                rnd = pe.snap(lay * ROUNDS + base_rnd)
                unit(rnd, 0, pe.snap(lay * LNS + 2 * which))
                with pe.Fori(0, FR - 1) as i:
                    one(i, True)
                one(FR - 1, False)

            pe.wait_ge(ident_landed, 16)
            pe.wait_ge(prepared, PREPARED)
            with pe.Fori(0, DEPTH) as lay:
                turn_x(pe.snap(lay * LNS), 0, (4, 5, 6, 7), down_added, lay * (2 * FR * 2 * TT) + BANKS)
                ffn_pe(lay, 0, 0)
                epoch = pe.snap(lay * LNS + 1)
                turn_x(epoch, LATENT_BANK, (4, 5, 6, 7), down_added, (lay * 2 + 1) * (FR * 2 * TT) + BANKS)
                rnd = pe.snap(lay * ROUNDS + FR)
                pe.wait_ge(xt_scaled, epoch * KB + 4)
                for s in range(UNITS):
                    split_unit(rnd, s)
                    for n in range(RG[s]):
                        k = RG0[s] + n
                        pe.wait_ge(xt_lo_done, epoch * KB + (k + 1))
                        for t in range(TT):
                            last = product(ps[:, LATENT_BANK + t, 0:LAT], xt(k, slice(t * P, (t + 1) * P)),
                                           w(s, slice(n * LAT, (n + 1) * LAT)), k == 0, k == KB - 1)
                            if k == KB - 1 and t < TT - 1:
                                last.then_inc(lat_out, 1)
                    last.then_inc(used[s], 1)

                def turn_latents():
                    pe.wait_ge(lat_scaled, (lay + 1) * (3 * TT))
                    for f, c0 in enumerate((0, P, 2 * P, LAT - P)):
                        for t in range(TT):
                            last = pe.transpose(ps[:, C_BANK[f], t * P:(t + 1) * P], c_tok[:, t, c0:c0 + P],
                                                ident[:])
                        last.then_inc(latT_out, 1)

                def turn_rms(hd):
                    pe.wait_ge(rb_done, hd + 1)
                    for t in range(TT):
                        last = pe.transpose(ps[:, 0, t * P:(t + 1) * P], rb[:, t, :], ident[:])
                    last.then_inc(rbT_out, 1)

                def out_sum(hd, rnd, b):
                    t, half = b // 2, slice((b % 2) * S, (b % 2 + 1) * S)
                    if b == 0:
                        split_unit(rnd, 4)
                        split_unit(rnd, 5)
                        pe.wait_ge(od_lo_done, hd + 2)
                        pe.wait_ge(om_lo_done, hd + 2)
                    if b >= 2:
                        pe.wait_ge(wo_added, hd * (2 * TT) + (BANKS + b - 1))
                    tok = slice(t * P, (t + 1) * P)
                    for j, (hi, lo) in enumerate(((od_hi, od_lo), (om_hi, om_lo))):
                        last = product(ps[:, b % 2, :], (hi[:, tok], lo[:, tok]), w(4 + j, half), j == 0, j == 1)
                        if b == 2 * TT - 1:
                            last.then_inc(used[4 + j], 1)
                        elif j == 1:
                            last.then_inc(wo_out, 1)

                def head(h, more):
                    rnd = pe.snap(h + (lay * ROUNDS + (FR + 1)))
                    hd = pe.snap(h + lay * HEADS)

                    def outs(*bs):
                        for b in bs:
                            if more:
                                out_sum(hd - 1, rnd - 1, b)

                    def bank_split(n):
                        pe.wait_ge(proj_lo, hd * 7 + n)

                    def d_scores(t):
                        tok = slice(t * P, (t + 1) * P)
                        for m in range(2):
                            if t >= 2:
                                pe.wait_ge(dbias, hd * (2 * TT) + (2 * t + m - 3))
                            product(ps[:, 2 + (2 * t + m) % 4, :], (qd_hi[:, tok], qd_lo[:, tok]),
                                    (kd_hi[:, m, :], kd_lo[:, m, :]), True, True).then_inc(dscore, 1)

                    def turn_a(n, src, ready, count):
                        pe.wait_ge(ready, count)
                        if n >= 2:
                            pe.wait_ge(at_lo, hd * (2 * TT) + (n - 1))
                        else:
                            bank_split(4 + 2 * n)
                        for j in range(TT):
                            last = pe.transpose(ps[:, 6 + n % 2, j * P:(j + 1) * P],
                                                src[:, j * P:(j + 1) * P], ident[:])
                        last.then_inc(at_out, 1)

                    def d_turn(t):
                        turn_a(t, prb[:, 2 * (t % 2), :], dnorm, hd * (3 * TT) + (3 * t + 3))

                    def m_turn(t):
                        turn_a(4 + t, prb[:, t, :], mnorm, hd * (2 * TT) + (2 * t + 2))

                    def pv(n, bank, v):
                        pe.wait_ge(at_lo, hd * (2 * TT) + (2 * n + 2))
                        for j in range(TT):
                            cols = slice(j * P, (j + 1) * P)
                            last = product(ps[:, bank, (n % 2) * HALF:(n % 2 + 1) * HALF],
                                           (v[0][:, cols], v[1][:, cols]),
                                           (a_hi[:, n % 2, j, :], a_lo[:, n % 2, j, :]), j == 0, j == TT - 1)
                        last.then_inc(pv_out, 1)

                    def m_scores(t):
                        tok = slice(t * P, (t + 1) * P)
                        pe.wait_ge(dbias, hd * (2 * TT) + (TT + t + 1))
                        if t == 0:
                            bank_split(6)
                            pe.wait_ge(rope_lo, h + (lay * (HEADS + 1) + 2))
                        product(ps[:, 2 + t, :], (qn_hi[:, tok], qn_lo[:, tok]), (kn_hi[:], kn_lo[:]), True, False)
                        product(ps[:, 2 + t, :], (qr_hi[:, tok], qr_lo[:, tok]), (kr_hi[:], kr_lo[:]),
                                False, True).then_inc(mscore, 1)

                    pe.wait_ge(mexp, hd * TT + BANKS)
                    for s, bank in enumerate((2, 3, 7)):
                        split_unit(rnd, s)
                        for k in range(KB):
                            last = product(ps[:, bank, :], w(s, slice(k * P, (k + 1) * P)), xt(k),
                                           k == 0, k == KB - 1)
                        last.then_inc(used[s], 1)
                        if s == 0 and more:
                            turn_rms(hd - 1)
                        if s == 1 and not more:
                            turn_latents()
                    pe.wait_ge(latT_lo, lay * 3 + 3)
                    pe.wait_ge(om_lo_done, hd + 1)
                    bank_split(3)
                    d_scores(0)
                    d_scores(1)
                    split_unit(rnd, 3)
                    pe.wait_ge(od_lo_done, hd + 1)
                    pe.wait_ge(rope_lo, h + (lay * (HEADS + 1) + 1))
                    for k in range(2):
                        last = product(ps[:, 0, :], w(3, slice(k * MQ + MQ - P, (k + 1) * MQ)),
                                       (c_hi[:, k, :], c_lo[:, k, :]), k == 0, k == 1)
                    last.then_inc(proj_out, 1)
                    pe.wait_ge(vt_copied, hd + 1)
                    for t in range(TT):
                        last = pe.transpose(ps[:, 6, t * P:(t + 1) * P], vt[:, t * P:(t + 1) * P], ident[:])
                    last.then_inc(vt_out, 1)
                    for k in range(2):
                        last = product(ps[:, 1, :], w(3, slice(k * MQ, k * MQ + NOPE)),
                                       (c_hi[:, k, :], c_lo[:, k, :]), k == 0, k == 1)
                    last.then_inc(proj_out, 1)
                    last = product(ps[:, 7, :], w(3, slice(2 * MQ, 2 * MQ + NOPE)),
                                   (c_hi[:, 2, :], c_lo[:, 2, :]), True, True)
                    last.then_inc(proj_out, 1)
                    pe.wait_ge(dbias, hd * (2 * TT) + 1)
                    for t in range(TT):
                        tok = slice(t * P, (t + 1) * P)
                        last = product(ps[:, 2, tok], (c_hi[:, 2, tok], c_lo[:, 2, tok]),
                                       w(3, slice(2 * MQ + NOPE, 2 * MQ + NOPE + VD)), True, True)
                    last.then_inc(used[3], 1)
                    pe.wait_ge(rope_swapped, 2 * h + (lay * (2 * (HEADS + 1)) + 4))
                    outs(0)
                    d_turn(0)
                    bank_split(7)
                    d_scores(2)
                    outs(1)
                    d_turn(1)
                    d_scores(3)
                    outs(2, 3)
                    d_turn(2)
                    outs(4)
                    m_scores(0)
                    outs(5)
                    d_turn(3)
                    m_scores(1)
                    m_scores(2)
                    outs(6, 7)
                    m_scores(3)
                    if more:
                        pe.wait_ge(wo_added, (hd - 1) * (2 * TT) + (BANKS + 7))
                    pv(0, 0, (vd_hi, vd_lo))
                    m_turn(0)
                    pv(1, 0, (vd_hi, vd_lo))
                    m_turn(1)
                    m_turn(2)
                    pe.wait_ge(sq_done, hd + 1)
                    pe.wait_ge(od_copied, hd + 1)
                    for t in range(TT):
                        last = pe.matmul(ps[:, 0, t:t + 1], sq[:, t * P:(t + 1) * P], ones[:], start=True,
                                         stop=True)
                    last.then_inc(ms_out, 1)
                    m_turn(3)
                    pe.wait_ge(mexp, hd * TT + (BANKS + 3))
                    pv(2, 4, (vm_hi, vm_lo))
                    pv(3, 4, (vm_hi, vm_lo))

                head(0, False)
                with pe.Fori(1, HEADS) as h:
                    head(h, True)
                rnd = pe.snap(lay * ROUNDS + (FR + HEADS))
                hd = pe.snap(lay * HEADS + (HEADS - 1))
                turn_rms(hd)
                for b in range(2 * TT):
                    out_sum(hd, rnd, b)
                turn_x(pe.snap(lay * LNS + 2), 0, (0, 1), wo_added, (lay + 1) * (HEADS * 2 * TT) + BANKS)
                ffn_pe(lay, 1, FR + 1 + HEADS)


_INS = ["x", "ffn1_w_gate", "ffn1_w_up", "ffn1_w_down", "ln1_g", "ln1_b", "w_in", "q_norm_g", "w_q_up",
        "kv_norm_g", "w_kv_up", "diff_lambda_q1", "diff_lambda_k1", "diff_lambda_q2", "diff_lambda_k2",
        "diff_subln_g", "w_out", "ln2_g", "ln2_b", "ffn2_w_gate", "ffn2_w_up", "ffn2_w_down", "ln3_g", "ln3_b"]


def constants():
    import math
    pos = np.arange(S, dtype=np.float32)
    inv = (np.float32(10000.0) ** (-np.arange(0, ROPE, 2, dtype=np.float32) / np.float32(ROPE))).astype(np.float32)
    ang = inv[:, None] * pos[None, :]
    c, s = np.cos(ang).astype(np.float32), np.sin(ang).astype(np.float32)
    part, col = np.arange(P)[:, None], np.arange(DIST)[None, :]
    init = [0.8 - 0.6 * math.exp(-0.3 * lay) for lay in range(DEPTH)]
    return {
        "ident": np.eye(P, dtype=np.float32),
        "alibi": (-(0.25 ** HEADS / DIFF_SCALE) * np.abs(part - col + (S - P))).astype(np.float32),
        "cos": np.concatenate([c, c]),
        "sin": np.concatenate([-s, s]),
        "lam": np.array([[v, 1.0 - v] for v in init], np.float32),
    }


def kernel(**inputs):
    import concourse.bacc as bacc
    from concourse.bass_utils import run_bass_kernel_spmd as run

    nc = bacc.Bacc("TRN2", target_bir_lowering=False, num_devices=1)
    arrays, args = {}, []
    for name in _INS:
        arrays[name] = np.ascontiguousarray(inputs[name])
    for name, a in constants().items():
        arrays["const_" + name] = a
    for name, a in arrays.items():
        args.append(nc.dram_tensor(name, a.shape, mybir.dt.from_np(a.dtype), kind="ExternalInput").ap())
    args.append(nc.dram_tensor("encoded", (1, S, D), F32, kind="ExternalOutput").ap())
    build(nc, *args)
    r = run(nc, [arrays], core_ids=[0])
    return r.results[0]["encoded"]
```

```python
from contextlib import ExitStack

import numpy as np
import concourse.bass as bass
from concourse import mybir

F32 = mybir.dt.float32
F32R = mybir.dt.float32r
ALU = mybir.AluOpType
ACT = mybir.ActivationFunctionType
AX = mybir.AxisListType

P = 128
D = 1024
S = 512
DEPTH = 2
F = 2816
HEADS = 4
NOPE, ROPE, VD = 128, 64, 128
QR, KVR = 256, 128
DH = 64
LAT = QR + KVR + ROPE
DQ0 = LAT
DK0 = DQ0 + HEADS * 2 * DH
DV0 = DK0 + HEADS * 2 * DH
EPS = 1e-5
ALPHA = (2 * DEPTH) ** 0.25
LN_EPS = EPS / ALPHA ** 2
KB = D // P
TT = S // P
FR = F // (2 * P)
UNITS = 6
RAW = 3
BANKS = 4
LATENT_BANK = 4
C_BANK = (6, 1, 4, 0)
POOL_TILE = 1
PREPARED = 14
RG = (2, 2, 1, 1, 1, 1)
RG0 = (0, 2, 4, 5, 6, 7)
ROUNDS = 2 * FR + 1 + HEADS
LNS = 3
MLA_SCALE = (NOPE + ROPE) ** -0.5
DIFF_SCALE = DH ** -0.5
DIST = S + S - P
HALF = S // 2


def build(nc, x, g1, u1, d1, ln1_g, ln1_b, w_in, q_norm_g, w_q_up, kv_norm_g, w_kv_up, lq1, lk1, lq2, lk2,
          subln_g, w_out, ln2_g, ln2_b, g2, u2, d2, ln3_g, ln3_b, c_ident, c_alibi, c_cos, c_sin, c_lam, out):
    ctx = ExitStack()
    with ctx:
        def sem(name):
            return ctx.enter_context(nc.semaphore(name))

        slab_bytes = nc.sbuf_usable_end - nc.sbuf_base - 64
        base = (nc.sbuf_base + 63) // 32 * 32
        ctx.enter_context(nc.sbuf_tensor("slab", [P, slab_bytes // 4 - 8], F32))
        top = [base]

        def size(shape):
            return int(np.prod(shape[1:])) * 4

        def at(offset, name, shape, dt=F32):
            assert offset + size(shape) <= base + slab_bytes, (name, offset + size(shape) - base - slab_bytes)
            return nc.alloc_sbuf_tensor_at(name, list(shape), dt, offset=offset)

        def sb(name, shape, dt=F32):
            t = at(top[0], name, shape, dt)
            top[0] += (size(shape) + 31) // 32 * 32
            return t

        def shared(*groups):
            start, end, made = top[0], top[0], []
            for group in groups:
                top[0] = start
                made += [sb(*one) for one in group]
                end = max(end, top[0])
            top[0] = end
            return made

        x_tok = sb("x_tok", [P, TT, D])
        x_hi = sb("x_hi", [P, KB, S], F32R)
        x_lo = sb("x_lo", [P, KB, S], F32R)
        raw = sb("raw", [P, RAW, D])
        w_hi = sb("w_hi", [P, UNITS, D], F32R)
        w_lo = sb("w_lo", [P, UNITS, D], F32R)
        (qd, vd_hi, vd_lo, qn_hi, qn_lo, kn_hi, kn_lo, vm_hi, vm_lo,
         silu, prod, h_hi, h_lo, xg) = shared(
            [("qd", [P, 2, S], F32R)] + [(n, [P, S], F32R) for n in ("vd_hi", "vd_lo", "qn_hi", "qn_lo",
                                         "kn_hi", "kn_lo", "vm_hi", "vm_lo")],
            [("silu", [P, 2, S], F32), ("prod", [P, 2, S], F32),
             ("h_hi", [P, 2, S], F32R), ("h_lo", [P, 2, S], F32R)],
            [("xg", [P, KB, S], F32)])
        kd_hi = sb("kd_hi", [P, 2, S], F32R)
        kd_lo = sb("kd_lo", [P, 2, S], F32R)
        qr = sb("qr", [P, S], F32R)
        kr_hi = sb("kr_hi", [P, S], F32R)
        kr_lo = sb("kr_lo", [P, S], F32R)
        c_hi, c_lo, ln_gb = shared([("c_hi", [P, 3, S], F32R), ("c_lo", [P, 3, S], F32R)],
                                   [("ln_gb", [P, 2, D], F32)])
        prb, c_tok, junk, lam_in, lam_junk = shared(
            [("prb", [P, 4, S], F32)],
            [("c_tok", [P, TT, LAT], F32), ("junk", [P, QR + KVR], F32)],
            [("lam_in", [P, 4, DH], F32), ("lam_junk", [P, 2, DH], F32)])
        a_hi = sb("a_hi", [P, 2, TT, HALF], F32R)
        a_lo = sb("a_lo", [P, 2, TT, HALF], F32R)
        od_hi = sb("od_hi", [P, S], F32R)
        od_lo = sb("od_lo", [P, S], F32R)
        om_hi = sb("om_hi", [P, S], F32R)
        om_lo = sb("om_lo", [P, S], F32R)
        od, sq, rb, rope_s, rope_w, vt, lat_g = shared(
            [("od", [P, S], F32), ("sq", [P, S], F32), ("rb", [P, TT, P], F32)],
            [("rope_s", [P, S], F32), ("rope_w", [P, S], F32), ("vt", [P, S], F32)],
            [("lat_g", [P, QR + KVR], F32)])
        alibi = sb("alibi", [P, DIST])
        cos = sb("cos", [P, S])
        sin = sb("sin", [P, S])
        ident = sb("ident", [P, P])
        lam_k = sb("lam_k", [P, 2])
        sub_g = sb("sub_g", [P, 1])
        sub_gs = sb("sub_gs", [P, 1])
        dots = sb("dots", [P, 2])
        edots = sb("edots", [P, 2])
        nlam = sb("nlam", [P, 2])
        ones = sb("ones", [P, 1])
        mhalf = sb("mhalf", [P, 8])
        wait_seat = sb("wait_seat", [P, 1])
        minus = sb("minus", [P, 1])
        ln_eps = sb("ln_eps", [P, 1])
        eps8 = sb("eps8", [P, 8])
        lat_n = sb("lat_n", [P, 8])
        gb_t = sb("gb_t", [P, 2, KB])
        nmean = sb("nmean", [P, TT])
        stats = sb("stats", [P, TT, 12])
        mv = sb("mv", [P, TT, 2])
        ve = sb("ve", [P, TT])
        rstd = sb("rstd", [P, TT])
        nmr = sb("nmr", [P, TT])
        ss = sb("ss", [P, 8])
        ssv = sb("ssv", [P, 8])
        rc = sb("rc", [P, 8])
        dmax = sb("dmax", [P, TT, 2])
        dneg = sb("dneg", [P, TT, 2])
        dsum = sb("dsum", [P, TT, 2])
        drec = sb("drec", [P, TT, 2])
        drl = sb("drl", [P, TT])
        mmax = sb("mmax", [P, TT])
        mneg = sb("mneg", [P, TT])
        msum = sb("msum", [P, TT])
        mrec = sb("mrec", [P, TT])
        ms = sb("ms", [P, TT])
        rms = sb("rms", [P, TT])

        ps = ctx.enter_context(nc.psum_tensor("ps", [P, 8, S], F32))

        const_landed = sem("const_landed")
        ident_landed = sem("ident_landed")
        x_landed = sem("x_landed")
        param_landed = sem("param_landed")
        gb_landed = sem("gb_landed")
        landed = [sem(f"landed{s}") for s in range(UNITS)]
        kvup_landed = sem("kvup_landed")
        stored = sem("stored")
        hi_done = [sem(f"hi_done{s}") for s in range(UNITS)]
        lo_done = [sem(f"lo_done{s}") for s in range(UNITS)]
        used = [sem(f"used{s}") for s in range(UNITS)]
        prepared = sem("prepared")
        silu_done, prod_done = sem("silu_done"), sem("prod_done")
        h_hi_done, h_lo_done = sem("h_hi_done"), sem("h_lo_done")
        down_out, down_added = sem("down_out"), sem("down_added")
        ln_stat, ln_agg, ln_pool = sem("ln_stat"), sem("ln_agg"), sem("ln_pool")
        ln_norm, ln_scaled = sem("ln_norm"), sem("ln_scaled")
        xt_out, xt_scaled, xt_lo_done = sem("xt_out"), sem("xt_scaled"), sem("xt_lo_done")
        pool_scaled = sem("pool_scaled")
        xt_hi_even, xt_hi_odd = sem("xt_hi_even"), sem("xt_hi_odd")
        lat_out, lat_sq, lat_pool, lat_scaled = sem("lat_out"), sem("lat_sq"), sem("lat_pool"), sem("lat_scaled")
        latT_out, latT_hi, latT_lo = sem("latT_out"), sem("latT_hi"), sem("latT_lo")
        rope_swapped, rope_cos, rope_sum = sem("rope_swapped"), sem("rope_cos"), sem("rope_sum")
        rope_hi, rope_lo, rope_twice = sem("rope_hi"), sem("rope_lo"), sem("rope_twice")
        lam_dot, lam_exp, lam_step = sem("lam_dot"), sem("lam_exp"), sem("lam_step")
        alibi_set = sem("alibi_set")
        proj_out, proj_hi, proj_lo = sem("proj_out"), sem("proj_hi"), sem("proj_lo")
        vt_copied, vt_out = sem("vt_copied"), sem("vt_out")
        dscore, dbias, dneg_done, dexp = sem("dscore"), sem("dbias"), sem("dneg_done"), sem("dexp")
        dscaled, dnorm = sem("dscaled"), sem("dnorm")
        mscore, mmax_done, mneg_done, mexp, mnorm = (sem("mscore"), sem("mmax_done"), sem("mneg_done"),
                                                     sem("mexp"), sem("mnorm"))
        at_out, at_hi, at_lo = sem("at_out"), sem("at_hi"), sem("at_lo")
        pv_out = sem("pv_out")
        od_copied, sq_done, ms_out, ms_copied, rms_done = (sem("od_copied"), sem("sq_done"), sem("ms_out"),
                                                           sem("ms_copied"), sem("rms_done"))
        rb_done, rbT_out, od_scaled, od_hi_done, od_lo_done = (sem("rb_done"), sem("rbT_out"), sem("od_scaled"),
                                                               sem("od_hi_done"), sem("od_lo_done"))
        om_hi_done, om_lo_done = sem("om_hi_done"), sem("om_lo_done")
        wo_out, wo_added = sem("wo_out"), sem("wo_added")

        def raw32(t):
            return t.bitcast(F32)

        def rows(w):
            return w.rearrange("(k p) f -> p k f", p=P)

        LAT_W = [n * LAT for n in RG]
        HEAD_W = [D, D, D, 2 * (NOPE + ROPE) + NOPE + VD, D, D]
        MQ = NOPE + ROPE

        block = ctx.enter_context(nc.Block())

        @block.sync
        def _(sp):
            def unit(rnd, s, dst_w, src, shape=None):
                if s < RAW:
                    sp.wait_ge(lo_done[s + RAW], rnd + 1)
                else:
                    sp.wait_ge(lo_done[s - RAW], rnd + 2)
                dst = raw[:, s % RAW, 0:dst_w]
                if shape is not None:
                    dst = dst.rearrange("p (k f) -> p k f", k=shape)
                sp.dma_start(dst, src).then_inc(landed[s], 16)

            def ffn_loads(lay, base_rnd, wg, wu, wd):
                with sp.Fori(0, FR) as i:
                    rnd = sp.snap(lay * ROUNDS + base_rnd + i)
                    for j in range(2):
                        cols = bass.ds(i * (2 * P) + j * P, P)
                        unit(rnd, 2 * j, D, rows(wg[lay])[:, :, cols], KB)
                        unit(rnd, 2 * j + 1, D, rows(wu[lay])[:, :, cols], KB)
                    for j in range(2):
                        unit(rnd, 4 + j, D, wd[lay, bass.ds(i * (2 * P) + j * P, P), :])

            def gb_load(lay, which, g, b):
                sp.wait_ge(ln_scaled, (lay * LNS + which + 1) * (2 * TT))
                sp.dma_start(ln_gb[:, 0, :], g[lay].partition_broadcast(P)).then_inc(gb_landed, 16)
                sp.dma_start(ln_gb[:, 1, :], b[lay].partition_broadcast(P)).then_inc(gb_landed, 16)
                sp.dma_start(gb_t[:, 0, :], g[lay].rearrange("(k p) -> p k", p=P),
                             allow_slow_non_contiguous=True).then_inc(gb_landed, 16)
                sp.dma_start(gb_t[:, 1, :], b[lay].rearrange("(k p) -> p k", p=P),
                             allow_slow_non_contiguous=True).then_inc(gb_landed, 16)

            for t in range(TT):
                sp.dma_start(x_tok[:, t, :], x[0, t * P:(t + 1) * P, :]).then_inc(x_landed, 16)
            sp.dma_start(ident[:], c_ident).then_inc(ident_landed, 16)
            with sp.Fori(0, DEPTH) as lay:
                ffn_loads(lay, 0, g1, u1, d1)
                sp.wait_ge(wo_added, lay * (HEADS * 2 * TT) + BANKS)
                sp.dma_start(alibi[:], c_alibi).then_inc(const_landed, 16)
                sp.dma_start(cos[P // 2:, :], c_cos).then_inc(const_landed, 16)
                sp.dma_start(sin[P // 2:, :], c_sin).then_inc(const_landed, 16)
                sp.dma_start(lat_g[:, 0:QR], q_norm_g[lay].partition_broadcast(P)).then_inc(param_landed, 16)
                sp.dma_start(lat_g[:, QR:], kv_norm_g[lay].partition_broadcast(P)).then_inc(param_landed, 16)
                for n, v in enumerate((lq1, lk1, lq2, lk2)):
                    sp.dma_start(lam_in[:, n, :], v[lay].partition_broadcast(P)).then_inc(param_landed, 16)
                sp.dma_start(lam_k[:], c_lam[lay].partition_broadcast(P)).then_inc(param_landed, 16)
                sp.dma_start(sub_g[:], subln_g[lay].rearrange("(p a) -> p a", a=1)).then_inc(param_landed, 16)
                gb_load(lay, 0, ln1_g, ln1_b)
                rnd = sp.snap(lay * ROUNDS + FR)
                for s in range(UNITS):
                    src = rows(w_in[lay])[:, RG0[s]:RG0[s] + RG[s], 0:LAT]
                    unit(rnd, s, LAT_W[s], src, RG[s])
                with sp.Fori(0, HEADS) as h:
                    rnd = sp.snap(lay * ROUNDS + (FR + 1) + h)
                    for s, c0 in enumerate((DQ0, DK0, DV0)):
                        unit(rnd, s, D, rows(w_in[lay])[:, :, bass.ds(h * P + c0, P)], KB)
                    unit(rnd, 3, 2 * MQ, rows(w_q_up[lay])[:, :, bass.ds(h * MQ, MQ)], 2)
                    sp.dma_start(raw[:, 0, 2 * MQ:2 * MQ + NOPE + VD],
                                 w_kv_up[lay, :, bass.ds(h * (NOPE + VD), NOPE + VD)]).then_inc(kvup_landed, 16)
                    unit(rnd, 4, D, w_out[lay, bass.ds(h * P + HEADS * VD, P), :])
                    unit(rnd, 5, D, w_out[lay, bass.ds(h * P, P), :])
                sp.wait_ge(proj_lo, (lay * HEADS + HEADS) * 8)
                gb_load(lay, 1, ln2_g, ln2_b)
                ffn_loads(lay, FR + 1 + HEADS, g2, u2, d2)
                gb_load(lay, 2, ln3_g, ln3_b)
            for n, t in enumerate([t for t in range(TT) if t != POOL_TILE] + [POOL_TILE]):
                if t == POOL_TILE:
                    sp.wait_ge(pool_scaled, 2)
                else:
                    sp.wait_ge(ln_scaled, DEPTH * LNS * 2 * TT + 2 * n + 2)
                sp.dma_start(out[0, t * P:(t + 1) * P, :], x_tok[:, t, :]).then_inc(stored, 16)
            sp.wait_ge(stored, 16 * TT)

        @block.gpsimd
        def _(pool):
            pool.memset(ones[:], 1.0).then_inc(prepared, 1)
            pool.memset(mhalf[:], -0.5).then_inc(prepared, 1)
            pool.memset(minus[:], -1.0).then_inc(prepared, 1)
            pool.memset(ln_eps[:], LN_EPS).then_inc(prepared, 1)
            pool.memset(eps8[:], EPS).then_inc(prepared, 1)
            pool.memset(lat_n[:, 0:TT], 1.0 / QR).then_inc(prepared, 1)
            pool.memset(lat_n[:, TT:], 1.0 / KVR).then_inc(prepared, 1)
            for z in (ln_gb, gb_t):
                pool.memset(z[:, 0, :], 1.0).then_inc(prepared, 1)
                pool.memset(z[:, 1, :], 0.0).then_inc(prepared, 1)
            pool.sem_inc(gb_landed, 64)
            for s in range(UNITS):
                pool.sem_inc(lo_done[s], 1)

            def lo_part(rnd, s, width):
                pool.wait_ge(hi_done[s], rnd + 1)
                pool.tensor_tensor(w_lo[:, s, 0:width], raw[:, s % RAW, 0:width], raw32(w_hi[:, s, 0:width]),
                                   ALU.subtract).then_inc(lo_done[s], 1)

            def ahead(rnd, widths):
                lo_part(rnd, 4, D)
                lo_part(rnd, 5, D)
                if widths is not None:
                    for s in range(4):
                        lo_part(rnd + 1, s, widths[s])

            def ffn_split(lay, base_rnd, after):
                with pool.Fori(0, FR - 1) as i:
                    ahead(pool.snap(lay * ROUNDS + base_rnd + i), [D] * 4)
                ahead(pool.snap(lay * ROUNDS + (base_rnd + FR - 1)), after)

            def ln_power(lay, w):
                ln = pool.snap(lay * LNS + w)
                for t in range(TT):
                    c = slice(t, t + 1)
                    pool.wait_ge(ln_agg, ln * TT + (t + 1))
                    pool.tensor_tensor(ve[:, c], mv[:, t, 1:2], ln_eps[:], ALU.add).then_inc(ln_pool, 1)
                    pool.tensor_tensor(nmean[:, c], mv[:, t, 0:1], minus[:], ALU.mult).then_inc(ln_pool, 1)
                    pool.wait_ge(ln_pool, ln * (4 * TT) + (4 * t + 2))
                    pool.tensor_tensor(rstd[:, c], ve[:, c], mhalf[:, 0:1], ALU.pow).then_inc(ln_pool, 1)
                    pool.wait_ge(ln_pool, ln * (4 * TT) + (4 * t + 3))
                    pool.tensor_tensor(nmr[:, c], nmean[:, c], rstd[:, c], ALU.mult).then_inc(ln_pool, 1)

            def rope(index, hi):
                both = slice(P // 2, P)
                pool.wait_ge(rope_swapped, index * 2 + 2)
                pool.tensor_tensor(rope_s[both, :], rope_s[both, :], sin[both, :], ALU.mult).then_inc(rope_sum, 1)
                pool.wait_ge(rope_sum, index * 2 + 1)
                pool.wait_ge(rope_cos, index + 1)
                pool.tensor_tensor(hi[both, :], rope_w[both, :], rope_s[both, :], ALU.add).then_inc(rope_hi, 1)
                pool.tensor_tensor(rope_w[both, :], rope_w[both, :], rope_s[both, :], ALU.add)\
                    .then_inc(rope_sum, 1)

            with pool.Fori(0, DEPTH) as lay:
                rnd = pool.snap(lay * ROUNDS)
                for s in range(4):
                    lo_part(rnd, s, D)
                ffn_split(lay, 0, LAT_W)
                ln_power(lay, 0)
                rnd = pool.snap(lay * ROUNDS + FR)
                for s in (4, 5):
                    lo_part(rnd, s, LAT_W[s])
                for s in range(4):
                    lo_part(rnd + 1, s, HEAD_W[s])
                pool.wait_ge(lat_sq, (lay + 1) * (2 * TT))
                pool.tensor_tensor(ssv[:], ss[:], lat_n[:], ALU.mult).then_inc(lat_pool, 1)
                pool.wait_ge(lat_pool, lay * 3 + 1)
                pool.tensor_tensor(ssv[:], ssv[:], eps8[:], ALU.add).then_inc(lat_pool, 1)
                pool.wait_ge(lat_pool, lay * 3 + 2)
                pool.tensor_tensor(rc[:], ssv[:], mhalf[:], ALU.pow).then_inc(lat_pool, 1)
                pool.wait_ge(const_landed, lay * 48 + 48)
                rope(lay * (HEADS + 1), kr_hi)

                def head(h, widths):
                    rnd = pool.snap(h + (lay * ROUNDS + (FR + 1)))
                    pool.wait_ge(lo_done[2], rnd + 2)
                    rope(pool.snap(h + (lay * (HEADS + 1) + 1)), qr)
                    lo_part(rnd + 1, 0, widths[0])
                    lo_part(rnd, 4, D)
                    lo_part(rnd, 5, D)
                    pool.wait_ge(ms_copied, lay * HEADS + h + 1)
                    pool.tensor_tensor(rms[:], ms[:], mhalf[:, 0:TT], ALU.pow).then_inc(rms_done, 1)
                    for s in (1, 3, 2):
                        lo_part(rnd + 1, s, widths[s])

                with pool.Fori(0, HEADS - 1) as h:
                    head(h, HEAD_W)
                head(HEADS - 1, [D] * 4)
                ln_power(lay, 1)
                ffn_split(lay, FR + 1 + HEADS, None)
                ln_power(lay, 2)
            xs = x_tok[:, POOL_TILE, :]
            pool.wait_ge(gb_landed, DEPTH * LNS * 64 + 64)
            pool.wait_ge(ln_norm, DEPTH * LNS * TT + POOL_TILE + 1)
            pool.tensor_tensor(xs, xs, ln_gb[:, 0, :], ALU.mult).then_inc(pool_scaled, 1)
            pool.wait_ge(pool_scaled, 1)
            pool.tensor_tensor(xs, xs, ln_gb[:, 1, :], ALU.add).then_inc(pool_scaled, 1)

        @block.scalar
        def _(act):
            def hi_part(rnd, s, width, also=None):
                act.wait_ge(landed[s], rnd * 16 + 16)
                if also is not None:
                    act.wait_ge(*also)
                act.wait_ge(used[s], rnd + 1)
                act.copy(w_hi[:, s, 0:width], raw[:, s % RAW, 0:width]).then_inc(hi_done[s], 1)

            def ffn_act(lay, which, base_rnd, after):
                def one(i, widths):
                    rnd = act.snap(i + (lay * ROUNDS + base_rnd))
                    ffn = act.snap(i + (lay * (2 * FR) + which * FR))

                    def silu_of(j):
                        act.wait_ge(used[2 * j], rnd + 2)
                        act.activation(silu[:, j, :], ps[:, 2 * j, :], ACT.Silu).then_inc(silu_done, 1)

                    def h_part(j):
                        act.wait_ge(prod_done, ffn * 2 + (j + 1))
                        act.wait_ge(used[5], rnd + 1)
                        act.copy(h_hi[:, j, :], prod[:, j, :]).then_inc(h_hi_done, 1)

                    def next_part(s):
                        if widths is not None:
                            hi_part(rnd + 1, s, widths[s])

                    silu_of(0)
                    hi_part(rnd, 4, D)
                    hi_part(rnd, 5, D)
                    h_part(0)
                    next_part(0)
                    next_part(1)
                    silu_of(1)
                    next_part(2)
                    h_part(1)
                    next_part(3)

                with act.Fori(0, FR - 1) as i:
                    one(i, [D] * 4)
                one(FR - 1, after)

            def norm(lay, which):
                ln = act.snap(lay * LNS + which)
                for t in range(TT):
                    act.wait_ge(ln_pool, ln * (4 * TT) + (4 * t + 4))
                    act.activation(x_tok[:, t, :], x_tok[:, t, :], ACT.Identity, bias=nmr[:, t:t + 1],
                                   scale=rstd[:, t:t + 1]).then_inc(ln_norm, 1)

            def turned(epoch, shift):
                act.wait_ge(gb_landed, epoch * 64 + 64)
                for k in range(KB):
                    act.wait_ge(xt_out, epoch * KB + (k + 1))
                    act.activation(xg[:, k, :], ps[:, (k + shift) % KB, :], ACT.Identity,
                                   bias=gb_t[:, 1, k:k + 1], scale=gb_t[:, 0, k:k + 1]).then_inc(xt_scaled, 1)
                    if k % 2 == 0:
                        act.wait_ge(xt_scaled, epoch * KB + (k + 1))
                        act.copy(x_hi[:, k, :], xg[:, k, :]).then_inc(xt_hi_even, 1)

            def swap_halves(index, bank):
                a, b = slice(P // 2, P // 2 + ROPE // 2), slice(P // 2 + ROPE // 2, P)
                act.wait_ge(rope_cos, index + 1)
                act.copy(rope_s[a, :], ps[b, bank, :]).then_inc(rope_swapped, 1)
                act.copy(rope_s[b, :], ps[a, bank, :]).then_inc(rope_swapped, 1)

            def head_unit(rnd, s, hd):
                hi_part(rnd, s, HEAD_W[s], also=(kvup_landed, hd * 16 + 16) if s == 3 else None)

            def head_units(rnd, hd):
                for s in range(4):
                    head_unit(rnd, s, hd)

            act.sem_inc(mexp, BANKS)
            act.wait_ge(prepared, PREPARED)
            act.wait_ge(x_landed, 16 * TT)
            act.sem_inc(ln_norm, TT)
            with act.Fori(0, DEPTH) as lay:
                rnd = act.snap(lay * ROUNDS)
                hi_part(rnd, 0, D)
                hi_part(rnd, 1, D)
                turned(act.snap(lay * LNS), 0)
                hi_part(rnd, 2, D)
                hi_part(rnd, 3, D)
                ffn_act(lay, 0, 0, LAT_W)
                norm(lay, 0)
                turned(act.snap(lay * LNS + 1), LATENT_BANK)
                rnd = act.snap(lay * ROUNDS + FR)
                for s in (4, 5):
                    hi_part(rnd, s, LAT_W[s])
                head_units(rnd + 1, lay * HEADS)
                act.wait_ge(lam_dot, lay * 2 + 2)
                act.activation(edots[:], dots[:], ACT.Exp).then_inc(lam_exp, 1)
                for t in range(TT):
                    if t < TT - 1:
                        act.wait_ge(lat_out, lay * (TT - 1) + (t + 1))
                    else:
                        act.wait_ge(used[5], rnd + 2)
                    if t > 0:
                        act.wait_ge(lat_sq, lay * (2 * TT) + 2 * t)
                    act.activation(junk[:, 0:QR], ps[:, LATENT_BANK + t, 0:QR], ACT.Square,
                                   accum_out=ss[:, t:t + 1]).then_inc(lat_sq, 1)
                    act.activation(junk[:, QR:], ps[:, LATENT_BANK + t, QR:QR + KVR], ACT.Square,
                                   accum_out=ss[:, TT + t:TT + t + 1]).then_inc(lat_sq, 1)
                swap_halves(lay * (HEADS + 1), C_BANK[3])
                act.wait_ge(ln_scaled, (lay * LNS + 2) * (2 * TT))
                for f in range(3):
                    act.wait_ge(latT_out, lay * 4 + (f + 2))
                    act.copy(c_hi[:, f, :], ps[:, C_BANK[f], :]).then_inc(latT_hi, 1)
                def head(h, more):
                    rnd = act.snap(h + (lay * ROUNDS + (FR + 1)))
                    hd = act.snap(h + lay * HEADS)

                    def unit_product(s):
                        act.wait_ge(used[s], rnd + 2)

                    def proj(dst, src):
                        act.copy(dst, src).then_inc(proj_hi, 1)

                    def next_part(s):
                        if more:
                            head_unit(rnd + 1, s, hd + 1)
                        else:
                            hi_part(rnd + 1, s, D)

                    def a_part(n):
                        act.wait_ge(at_out, hd * (2 * TT) + (n + 1))
                        if n % 2 == 0:
                            act.wait_ge(pv_out, hd * 4 + (n // 2 + 1))
                        act.copy(a_hi[:, n // 2 % 2, :, (n % 2) * P:(n % 2 + 1) * P],
                                 ps[:, 6 + n % 2, :].rearrange("p (j q) -> p j q", j=TT)).then_inc(at_hi, 1)

                    def d_exp(t):
                        act.wait_ge(dneg_done, hd * TT + (t + 1))
                        for m in range(2):
                            p = prb[:, 2 * (t % 2) + m, :]
                            act.activation(p, p, ACT.Exp, bias=dneg[:, t, m:m + 1],
                                           accum_out=dsum[:, t, m:m + 1]).then_inc(dexp, 1)

                    def d_scale(t):
                        act.wait_ge(dnorm, hd * (3 * TT) + (3 * t + 1))
                        p1 = prb[:, 2 * (t % 2), :]
                        act.activation(p1, p1, ACT.Copy, scale=drec[:, t, 0:1]).then_inc(dscaled, 1)

                    def m_exp(t):
                        act.wait_ge(mneg_done, hd * TT + (t + 1))
                        act.wait_ge(at_out, hd * (2 * TT) + (3 + t // 2))
                        act.activation(prb[:, t, :], ps[:, 2 + t, :], ACT.Exp, bias=mneg[:, t:t + 1],
                                       scale=MLA_SCALE, accum_out=msum[:, t:t + 1]).then_inc(mexp, 1)

                    unit_product(0)
                    for m in range(2):
                        own = slice(m * DH, (m + 1) * DH)
                        proj(qd[own, m, :], ps[own, 2, :])
                    unit_product(1)
                    for m in range(2):
                        own, other = slice(m * DH, (m + 1) * DH), slice((1 - m) * DH, (2 - m) * DH)
                        proj(kd_hi[own, m, :], ps[own, 3, :])
                        proj(kd_hi[other, m, :], ps[own, 3, :])
                    swap_halves(h + (lay * (HEADS + 1) + 1), 0)
                    act.wait_ge(proj_out, hd * 3 + 2)
                    proj(qn_hi[:], ps[:, 1, :])
                    act.wait_ge(proj_out, hd * 3 + 3)
                    proj(kn_hi[:], ps[:, 6, :])
                    d_exp(0)
                    d_scale(0)
                    d_exp(1)
                    d_scale(1)
                    unit_product(2)
                    act.copy(vt[:], ps[:, 7, :]).then_inc(vt_copied, 1)
                    a_part(0)
                    act.wait_ge(vt_out, hd + 1)
                    proj(vd_hi[:], ps[:, 0, :])
                    d_exp(2)
                    a_part(1)
                    unit_product(3)
                    proj(vm_hi[:], ps[:, 1, :])
                    d_scale(2)
                    d_exp(3)
                    d_scale(3)
                    a_part(2)
                    m_exp(0)
                    next_part(0)
                    a_part(3)
                    m_exp(1)
                    m_exp(2)
                    m_exp(3)
                    hi_part(rnd, 4, D)
                    a_part(4)
                    act.wait_ge(pv_out, hd * 4 + (2 + 2))
                    act.activation(sq[:], ps[:, 0, :], ACT.Square).then_inc(sq_done, 1)
                    act.copy(od[:], ps[:, 0, :]).then_inc(od_copied, 1)
                    a_part(5)
                    hi_part(rnd, 5, D)
                    a_part(6)
                    a_part(7)
                    act.wait_ge(pv_out, hd * 4 + (2 + 4))
                    act.copy(om_hi[:], ps[:, 4, :]).then_inc(om_hi_done, 1)
                    next_part(1)
                    act.wait_ge(od_scaled, hd + 1)
                    act.copy(od_hi[:], od[:]).then_inc(od_hi_done, 1)
                    next_part(3)
                    next_part(2)

                with act.Fori(0, HEADS - 1) as h:
                    head(h, True)
                head(HEADS - 1, False)
                norm(lay, 1)
                turned(act.snap(lay * LNS + 2), 0)
                ffn_act(lay, 1, FR + 1 + HEADS, None)
                norm(lay, 2)

        @block.vector
        def _(dve):
            def rest(lo, src, hi):
                return dve.tensor_tensor(lo, src, raw32(hi), ALU.subtract)

            def add_and_stat(ln, add, added, count):
                def half_stat(b):
                    t, half = b // 2, b % 2
                    dve.wait_ge(added, count + (b + 1))
                    dve.bn_stats(stats[:, t, 6 * half:6 * half + 6], x_tok[:, t, half * S:(half + 1) * S])\
                        .then_inc(ln_stat, 1)

                def aggregate(t):
                    dve.wait_ge(ln_stat, ln * (2 * TT) + (2 * t + 2))
                    dve.memset(wait_seat[:], 0.0)
                    dve.bn_aggr(mv[:, t, :], stats[:, t, :]).then_inc(ln_agg, 1)

                for b in range(2 * TT):
                    add(b)
                    if b > 0:
                        half_stat(b - 1)
                    if b > 1 and b % 2 == 1:
                        aggregate(b // 2 - 1)
                half_stat(2 * TT - 1)
                aggregate(TT - 1)

            def turned_lo(epoch):
                for k in range(KB):
                    dve.wait_ge(xt_scaled, epoch * KB + (k + 1))
                    if k % 2 == 0:
                        dve.wait_ge(xt_hi_even, epoch * (KB // 2) + (k // 2 + 1))
                    else:
                        dve.tensor_copy(x_hi[:, k, :], xg[:, k, :]).then_inc(xt_hi_odd, 1)
                        dve.wait_ge(xt_hi_odd, epoch * (KB // 2) + (k // 2 + 1))
                    rest(x_lo[:, k, :], xg[:, k, :], x_hi[:, k, :]).then_inc(xt_lo_done, 1)

            def gains(epoch, tiles=range(TT)):
                dve.wait_ge(gb_landed, epoch * 64 + 64)
                for n, t in enumerate(tiles):
                    dve.wait_ge(ln_norm, epoch * TT + (t + 1))
                    xs = x_tok[:, t, :]
                    dve.tensor_tensor(xs, xs, ln_gb[:, 0, :], ALU.mult).then_inc(ln_scaled, 1)
                    dve.wait_ge(ln_scaled, epoch * (2 * TT) + (2 * n + 1))
                    dve.tensor_tensor(xs, xs, ln_gb[:, 1, :], ALU.add).then_inc(ln_scaled, 1)

            def ffn_dve(lay, which):
                def one(i, last):
                    rnd = dve.snap(i + (lay * ROUNDS + (which * (FR + 1 + HEADS))))
                    ffn = dve.snap(i + (lay * (2 * FR) + which * FR))
                    for j in range(2):
                        dve.wait_ge(silu_done, ffn * 2 + (j + 1))
                        dve.wait_ge(used[2 * j + 1], rnd + 2)
                        dve.tensor_tensor(prod[:, j, :], ps[:, 2 * j + 1, :], silu[:, j, :], ALU.mult)\
                            .then_inc(prod_done, 1)
                        dve.wait_ge(h_hi_done, ffn * 2 + (j + 1))
                        rest(h_lo[:, j, :], prod[:, j, :], h_hi[:, j, :]).then_inc(h_lo_done, 1)

                    def add(b):
                        if b == 0:
                            dve.wait_ge(down_added, ffn * (2 * TT) + BANKS)
                            dve.wait_ge(ln_scaled, (lay * LNS + (2 * which + 1)) * (2 * TT))
                        xs = x_tok[:, b // 2, (b % 2) * S:(b % 2 + 1) * S]
                        if b < 2 * TT - 1:
                            dve.wait_ge(down_out, ffn * (2 * TT - 1) + (b + 1))
                        else:
                            dve.wait_ge(used[5], rnd + 2)
                        dve.scalar_tensor_tensor(xs, ps[:, 4 + b % 4, :], 0.5 / ALPHA, xs, ALU.mult, ALU.add)\
                            .then_inc(down_added, 1)

                    if last:
                        add_and_stat(dve.snap(lay * LNS + 2 * which), add, down_added, ffn * (2 * TT) + BANKS)
                    else:
                        for b in range(2 * TT):
                            add(b)

                with dve.Fori(0, FR - 1) as i:
                    one(i, False)
                one(FR - 1, True)

            def rope(bank):
                both = slice(P // 2, P)
                dve.tensor_tensor(rope_w[both, :], ps[both, bank, :], cos[both, :], ALU.mult)\
                    .then_inc(rope_cos, 1)

            def rope_rest(index, lo, hi):
                dve.wait_ge(rope_hi, index + 1)
                dve.wait_ge(rope_sum, index * 2 + 2)
                rest(lo, rope_w[P // 2:P, :], hi).then_inc(rope_lo, 1)

            dve.sem_inc(down_added, BANKS)
            dve.sem_inc(wo_added, BANKS)
            dve.sem_inc(od_lo_done, 1)
            dve.sem_inc(om_lo_done, 1)
            for z in (kd_lo[P // 2:P, 0, :], kd_lo[0:P // 2, 1, :], kr_lo[0:P // 2, :]):
                dve.memset(raw32(z), 0.0).then_inc(prepared, 1)
            dve.sem_inc(alibi_set, 1)
            dve.wait_ge(prepared, PREPARED)
            with dve.Fori(0, DEPTH) as lay:
                turned_lo(dve.snap(lay * LNS))
                gains(dve.snap(lay * LNS))
                ffn_dve(lay, 0)
                turned_lo(dve.snap(lay * LNS + 1))
                gains(dve.snap(lay * LNS + 1))
                dve.wait_ge(param_landed, lay * 128 + 128)
                for n in range(2):
                    dve.tensor_tensor_reduce(lam_junk[:, n, :], lam_in[:, 2 * n, :], lam_in[:, 2 * n + 1, :], 1.0, 0.0,
                                             ALU.mult, ALU.add, dots[:, n:n + 1]).then_inc(lam_dot, 1)
                dve.tensor_tensor(sub_gs[:], sub_g[:], lam_k[:, 1:2], ALU.mult).then_inc(lam_step, 1)
                dve.wait_ge(lam_exp, lay + 1)
                dve.tensor_tensor(nlam[:, 0:1], edots[:, 1:2], edots[:, 0:1], ALU.subtract).then_inc(lam_step, 1)
                dve.wait_ge(lam_step, lay * 3 + 2)
                dve.tensor_tensor(nlam[:, 1:2], nlam[:, 0:1], lam_k[:, 0:1], ALU.subtract).then_inc(lam_step, 1)
                for t in range(TT):
                    dve.wait_ge(lat_sq, lay * (2 * TT) + (2 * t + 2))
                    dve.tensor_copy(c_tok[:, t, QR + KVR:], ps[:, LATENT_BANK + t, QR + KVR:LAT]).then_inc(lat_scaled, 1)
                dve.wait_ge(lat_pool, lay * 3 + 3)
                for t in range(TT):
                    dve.scalar_tensor_tensor(c_tok[:, t, 0:QR], ps[:, LATENT_BANK + t, 0:QR], rc[:, t:t + 1], lat_g[:, 0:QR],
                                             ALU.mult, ALU.mult).then_inc(lat_scaled, 1)
                    dve.scalar_tensor_tensor(c_tok[:, t, QR:QR + KVR], ps[:, LATENT_BANK + t, QR:QR + KVR],
                                             rc[:, TT + t:TT + t + 1], lat_g[:, QR:], ALU.mult, ALU.mult)\
                        .then_inc(lat_scaled, 1)
                dve.wait_ge(latT_out, lay * 4 + 1)
                dve.wait_ge(const_landed, lay * 48 + 48)
                rope(C_BANK[3])
                for f in range(3):
                    dve.wait_ge(latT_hi, lay * 3 + (f + 1))
                    rest(c_lo[:, f, :], ps[:, C_BANK[f], :], c_hi[:, f, :]).then_inc(latT_lo, 1)
                def add_out(hd, rnd, b):
                    if b == 0:
                        dve.wait_ge(wo_added, hd * (2 * TT) + BANKS)
                        dve.wait_ge(ln_scaled, (lay * LNS + 2) * (2 * TT))
                    xs = x_tok[:, b // 2, (b % 2) * S:(b % 2 + 1) * S]
                    if b < 2 * TT - 1:
                        dve.wait_ge(wo_out, hd * (2 * TT - 1) + (b + 1))
                    else:
                        dve.wait_ge(used[5], rnd + 2)
                    dve.scalar_tensor_tensor(xs, ps[:, b % 2, :], 1.0 / ALPHA, xs, ALU.mult, ALU.add)\
                        .then_inc(wo_added, 1)

                def head(h, more):
                    rnd = dve.snap(h + (lay * ROUNDS + (FR + 1)))
                    hd = dve.snap(h + lay * HEADS)

                    def outs(*bs):
                        for b in bs:
                            if more:
                                add_out(hd - 1, rnd - 1, b)

                    def proj(n_hi, lo, src, hi):
                        dve.wait_ge(proj_hi, hd * 10 + n_hi)
                        rest(lo, src, hi).then_inc(proj_lo, 1)

                    def d_bias(t):
                        if t >= 2:
                            dve.wait_ge(at_out, hd * (2 * TT) + (t - 1))
                        if t == 0:
                            dve.wait_ge(alibi_set, hd + 2)
                        dve.wait_ge(dscore, hd * (2 * TT) + (2 * t + 2))
                        dve.memset(wait_seat[:], 0.0)
                        for m in range(2):
                            off = (TT - 1 - t) * P
                            dve.tensor_tensor_reduce(prb[:, 2 * (t % 2) + m, :], ps[:, 2 + (2 * t + m) % 4, :],
                                                     alibi[:, off:off + S], DIFF_SCALE, -3.0e38, ALU.add, ALU.max,
                                                     dmax[:, t, m:m + 1]).then_inc(dbias, 1)
                        dve.wait_ge(dbias, hd * (2 * TT) + (2 * t + 2))
                        dve.tensor_scalar(dneg[:, t, :], dmax[:, t, :], -1.0, None, ALU.mult)\
                            .then_inc(dneg_done, 1)

                    def d_recs(t):
                        dve.wait_ge(dexp, hd * (2 * TT) + (2 * t + 2))
                        dve.reciprocal(drec[:, t, :], dsum[:, t, :]).then_inc(dnorm, 1)
                        dve.wait_ge(dnorm, hd * (3 * TT) + (3 * t + 1))
                        dve.tensor_scalar(drl[:, t:t + 1], drec[:, t, 1:2], nlam[:, 1:2], None, ALU.mult)\
                            .then_inc(dnorm, 1)

                    def d_norm(t):
                        p1, p2 = prb[:, 2 * (t % 2), :], prb[:, 2 * (t % 2) + 1, :]
                        dve.wait_ge(dscaled, hd * TT + (t + 1))
                        dve.wait_ge(dnorm, hd * (3 * TT) + (3 * t + 2))
                        dve.scalar_tensor_tensor(p1, p2, drl[:, t:t + 1], p1, ALU.mult, ALU.add)\
                            .then_inc(dnorm, 1)

                    def a_rest(n):
                        dve.wait_ge(at_hi, hd * (2 * TT) + (n + 1))
                        q = slice((n % 2) * P, (n % 2 + 1) * P)
                        rest(a_lo[:, n // 2 % 2, :, q], ps[:, 6 + n % 2, :].rearrange("p (j q) -> p j q", j=TT),
                             a_hi[:, n // 2 % 2, :, q]).then_inc(at_lo, 1)

                    def m_max(t):
                        dve.wait_ge(mscore, hd * TT + (t + 1))
                        dve.tensor_reduce(mmax[:, t:t + 1], ps[:, 2 + t, :], AX.X, ALU.max)\
                            .then_inc(mmax_done, 1)
                        dve.wait_ge(mmax_done, hd * TT + (t + 1))
                        dve.tensor_scalar(mneg[:, t:t + 1], mmax[:, t:t + 1], -MLA_SCALE, None, ALU.mult)\
                            .then_inc(mneg_done, 1)

                    def m_norm(t):
                        dve.wait_ge(mexp, hd * TT + (BANKS + t + 1))
                        dve.reciprocal(mrec[:, t:t + 1], msum[:, t:t + 1]).then_inc(mnorm, 1)
                        dve.wait_ge(mnorm, hd * (2 * TT) + (2 * t + 1))
                        dve.tensor_scalar(prb[:, t, :], prb[:, t, :], mrec[:, t:t + 1], None, ALU.mult)\
                            .then_inc(mnorm, 1)

                    dve.wait_ge(alibi_set, hd + 1)
                    dve.tensor_scalar(alibi[:], alibi[:], 0.25, None, ALU.mult).then_inc(alibi_set, 1)
                    for m in range(2):
                        own, other = slice(m * DH, (m + 1) * DH), slice((1 - m) * DH, (2 - m) * DH)
                        proj(2, qd[other, m, :], ps[own, 2, :], qd[own, m, :])
                    if not more:
                        high, low = slice(P // 2, P), slice(0, P // 2)
                        rope_rest(lay * (HEADS + 1), kr_lo[high, :], kr_hi[high, :])
                        dve.tensor_copy(kr_hi[low, :], raw32(kr_hi[high, :])).then_inc(rope_twice, 1)
                    for m in range(2):
                        own = slice(m * DH, (m + 1) * DH)
                        proj(6, kd_lo[own, m, :], ps[own, 3, :], kd_hi[own, m, :])
                    dve.wait_ge(proj_out, hd * 3 + 1)
                    rope(0)
                    d_bias(0)
                    d_bias(1)
                    proj(7, qn_lo[:], ps[:, 1, :], qn_hi[:])
                    d_recs(0)
                    proj(8, kn_lo[:], ps[:, 6, :], kn_hi[:])
                    d_norm(0)
                    d_recs(1)
                    d_norm(1)
                    rope_rest(h + (lay * (HEADS + 1) + 1), qr[0:P // 2, :], qr[P // 2:P, :])
                    d_bias(2)
                    a_rest(0)
                    proj(9, vd_lo[:], ps[:, 0, :], vd_hi[:])
                    d_bias(3)
                    d_recs(2)
                    proj(10, vm_lo[:], ps[:, 1, :], vm_hi[:])
                    a_rest(1)
                    d_norm(2)
                    outs(0)
                    d_recs(3)
                    outs(1)
                    d_norm(3)
                    a_rest(2)
                    m_max(0)
                    outs(2)
                    a_rest(3)
                    m_max(1)
                    outs(3)
                    m_max(2)
                    m_norm(0)
                    outs(4)
                    m_norm(1)
                    outs(5)
                    m_max(3)
                    m_norm(2)
                    outs(6)
                    outs(7)
                    m_norm(3)
                    a_rest(4)
                    a_rest(5)
                    dve.wait_ge(ms_out, hd + 1)
                    dve.tensor_scalar(ms[:], ps[:, 0, 0:TT], 1.0 / (2 * DH), EPS, ALU.mult, ALU.add)\
                        .then_inc(ms_copied, 1)
                    a_rest(6)
                    a_rest(7)
                    dve.wait_ge(rms_done, hd + 1)
                    dve.tensor_copy(rb[:], rms[:].rearrange("p (t a) -> p t a", a=1).to_broadcast([P, TT, P]))\
                        .then_inc(rb_done, 1)
                    dve.wait_ge(om_hi_done, hd + 1)
                    rest(om_lo[:], ps[:, 4, :], om_hi[:]).then_inc(om_lo_done, 1)
                    dve.wait_ge(rbT_out, hd + 1)
                    dve.scalar_tensor_tensor(od[:], ps[:, 0, :], sub_gs[:], od[:], ALU.mult, ALU.mult)\
                        .then_inc(od_scaled, 1)
                    dve.wait_ge(od_hi_done, hd + 1)
                    rest(od_lo[:], od[:], od_hi[:]).then_inc(od_lo_done, 1)

                head(0, False)
                with dve.Fori(1, HEADS) as h:
                    head(h, True)
                rnd = dve.snap(lay * ROUNDS + (FR + HEADS))
                hd = dve.snap(lay * HEADS + (HEADS - 1))
                add_and_stat(dve.snap(lay * LNS + 1), lambda b: add_out(hd, rnd, b), wo_added,
                             hd * (2 * TT) + BANKS)
                turned_lo(dve.snap(lay * LNS + 2))
                gains(dve.snap(lay * LNS + 2))
                ffn_dve(lay, 1)
            gains(DEPTH * LNS, [t for t in range(TT) if t != POOL_TILE])

        @block.tensor
        def _(pe):
            for s in range(UNITS):
                pe.sem_inc(used[s], 1)
            pe.sem_inc(pv_out, 2)

            def product(out, left, right, first, last):
                pe.matmul(out, left[0], right[0], start=first, stop=False)
                pe.matmul(out, left[0], right[1], start=False, stop=False)
                return pe.matmul(out, left[1], right[0], start=False, stop=last)

            def split_unit(rnd, s):
                pe.wait_ge(lo_done[s], rnd + 2)

            def w(s, cols):
                return w_hi[:, s, cols], w_lo[:, s, cols]

            def xt(k, q=slice(0, S)):
                return x_hi[:, k, q], x_lo[:, k, q]

            def turn_x(epoch, shift, late_banks, added, count):
                def turn(t, k):
                    return pe.transpose(ps[:, (k + shift) % KB, t * P:(t + 1) * P],
                                        x_tok[:, t, k * P:(k + 1) * P], ident[:])

                late = [k for k in range(KB) if (k + shift) % KB in late_banks]
                for t in range(2):
                    pe.wait_ge(ln_norm, epoch * TT + (t + 1))
                    for k in range(KB):
                        if k not in late:
                            turn(t, k)
                pe.wait_ge(added, count)
                for t in range(2):
                    for k in late:
                        turn(t, k)
                for t in range(2, TT - 1):
                    pe.wait_ge(ln_norm, epoch * TT + (t + 1))
                    for k in range(KB):
                        turn(t, k)
                pe.wait_ge(ln_norm, epoch * TT + TT)
                for k in range(KB):
                    turn(TT - 1, k).then_inc(xt_out, 1)

            def down_rows(rnd, ffn, last_round):
                def part(b, j):
                    tok = slice((b // 2) * P, (b // 2 + 1) * P)
                    return product(ps[:, 4 + b % 4, :], (h_hi[:, j, tok], h_lo[:, j, tok]),
                                   w(4 + j, slice((b % 2) * S, (b % 2 + 1) * S)), j == 0, j == 1)

                split_unit(rnd, 4)
                split_unit(rnd, 5)
                if last_round:
                    pe.wait_ge(h_lo_done, ffn * 2 + 1)
                    for b in range(4):
                        pe.wait_ge(down_added, ffn * (2 * TT) + (b + 1))
                        part(b, 0)
                pe.wait_ge(h_lo_done, ffn * 2 + 2)
                for b in range(2 * TT):
                    if not (last_round and b < 4):
                        pe.wait_ge(down_added, ffn * (2 * TT) + (b + 1))
                        first = part(b, 0)
                        if b == 2 * TT - 1:
                            first.then_inc(used[4], 1)
                    last = part(b, 1)
                    last.then_inc(used[5] if b == 2 * TT - 1 else down_out, 1)

            def ffn_pe(lay, which, base_rnd):
                def column(s, k):
                    return product(ps[:, s, :], w(s, slice(k * P, (k + 1) * P)), xt(k), k == 0, k == KB - 1)

                def unit(rnd, s):
                    split_unit(rnd, s)
                    for k in range(KB):
                        last = column(s, k)
                    last.then_inc(used[s], 1)

                def one(i, more):
                    rnd = pe.snap(i + (lay * ROUNDS + base_rnd))
                    ffn = pe.snap(i + (lay * (2 * FR) + which * FR))
                    unit(rnd, 2)
                    unit(rnd, 3)
                    if more:
                        pe.wait_ge(silu_done, ffn * 2 + 1)
                        unit(rnd + 1, 0)
                        pe.wait_ge(prod_done, ffn * 2 + 1)
                        unit(rnd + 1, 1)
                    down_rows(rnd, ffn, not more)

                rnd = pe.snap(lay * ROUNDS + base_rnd)
                epoch = pe.snap(lay * LNS + 2 * which)
                split_unit(rnd, 0)
                split_unit(rnd, 1)
                for k in range(KB):
                    pe.wait_ge(xt_lo_done, epoch * KB + (k + 1))
                    gate = column(0, k)
                    if k == 0:
                        pe.wait_ge(xt_scaled, epoch * KB + 2)
                    up = column(1, k)
                gate.then_inc(used[0], 1)
                up.then_inc(used[1], 1)
                with pe.Fori(0, FR - 1) as i:
                    one(i, True)
                one(FR - 1, False)

            pe.wait_ge(ident_landed, 16)
            pe.wait_ge(prepared, PREPARED)
            with pe.Fori(0, DEPTH) as lay:
                turn_x(pe.snap(lay * LNS), 0, (4, 5, 6, 7), down_added, lay * (2 * FR * 2 * TT) + BANKS)
                ffn_pe(lay, 0, 0)
                epoch = pe.snap(lay * LNS + 1)
                turn_x(epoch, LATENT_BANK, (4, 5, 6, 7), down_added, (lay * 2 + 1) * (FR * 2 * TT) + BANKS)
                rnd = pe.snap(lay * ROUNDS + FR)
                for s in range(UNITS):
                    split_unit(rnd, s)
                    for n in range(RG[s]):
                        k = RG0[s] + n
                        pe.wait_ge(xt_lo_done, epoch * KB + (k + 1))
                        for t in range(TT):
                            if k == 0:
                                pe.wait_ge(xt_scaled, epoch * KB + (t + 1))
                            last = product(ps[:, LATENT_BANK + t, 0:LAT], xt(k, slice(t * P, (t + 1) * P)),
                                           w(s, slice(n * LAT, (n + 1) * LAT)), k == 0, k == KB - 1)
                            if k == KB - 1 and t < TT - 1:
                                last.then_inc(lat_out, 1)
                    last.then_inc(used[s], 1)

                def turn_latents():
                    pe.wait_ge(lat_scaled, (lay + 1) * (3 * TT))
                    for f, c0 in ((3, LAT - P), (0, 0), (1, P), (2, 2 * P)):
                        for t in range(TT):
                            last = pe.transpose(ps[:, C_BANK[f], t * P:(t + 1) * P], c_tok[:, t, c0:c0 + P],
                                                ident[:])
                        last.then_inc(latT_out, 1)

                def turn_rms(hd):
                    pe.wait_ge(rb_done, hd + 1)
                    for t in range(TT):
                        last = pe.transpose(ps[:, 0, t * P:(t + 1) * P], rb[:, t, :], ident[:])
                    last.then_inc(rbT_out, 1)

                def out_sum(hd, rnd, b):
                    t, half = b // 2, slice((b % 2) * S, (b % 2 + 1) * S)
                    if b == 0:
                        split_unit(rnd, 4)
                        split_unit(rnd, 5)
                        pe.wait_ge(od_lo_done, hd + 2)
                        pe.wait_ge(om_lo_done, hd + 2)
                    if b >= 2:
                        pe.wait_ge(wo_added, hd * (2 * TT) + (BANKS + b - 1))
                    tok = slice(t * P, (t + 1) * P)
                    for j, (hi, lo) in enumerate(((od_hi, od_lo), (om_hi, om_lo))):
                        last = product(ps[:, b % 2, :], (hi[:, tok], lo[:, tok]), w(4 + j, half), j == 0, j == 1)
                        if b == 2 * TT - 1:
                            last.then_inc(used[4 + j], 1)
                        elif j == 1:
                            last.then_inc(wo_out, 1)

                def head(h, more):
                    rnd = pe.snap(h + (lay * ROUNDS + (FR + 1)))
                    hd = pe.snap(h + lay * HEADS)

                    def outs(*bs):
                        for b in bs:
                            if more:
                                out_sum(hd - 1, rnd - 1, b)

                    def bank_split(n):
                        pe.wait_ge(proj_lo, hd * 8 + n)

                    def d_scores(t):
                        tok = slice(t * P, (t + 1) * P)
                        for m in range(2):
                            if t >= 2:
                                pe.wait_ge(dbias, hd * (2 * TT) + (2 * t + m - 3))
                            scores = ps[:, 2 + (2 * t + m) % 4, :]
                            pe.matmul(scores, qd[:, m, tok], kd_hi[:, m, :], start=True, stop=False)
                            pe.matmul(scores, qd[:, m, tok], kd_lo[:, m, :], start=False, stop=True)\
                                .then_inc(dscore, 1)

                    def turn_a(n, src, ready, count):
                        pe.wait_ge(ready, count)
                        if n >= 2:
                            pe.wait_ge(at_lo, hd * (2 * TT) + (n - 1))
                        for j in range(TT):
                            last = pe.transpose(ps[:, 6 + n % 2, j * P:(j + 1) * P],
                                                src[:, j * P:(j + 1) * P], ident[:])
                        last.then_inc(at_out, 1)

                    def d_turn(t):
                        turn_a(t, prb[:, 2 * (t % 2), :], dnorm, hd * (3 * TT) + (3 * t + 3))

                    def m_turn(t):
                        turn_a(4 + t, prb[:, t, :], mnorm, hd * (2 * TT) + (2 * t + 2))

                    def pv(n, bank, v):
                        pe.wait_ge(at_lo, hd * (2 * TT) + (2 * n + 2))
                        for j in range(TT):
                            cols = slice(j * P, (j + 1) * P)
                            last = product(ps[:, bank, (n % 2) * HALF:(n % 2 + 1) * HALF],
                                           (v[0][:, cols], v[1][:, cols]),
                                           (a_hi[:, n % 2, j, :], a_lo[:, n % 2, j, :]), j == 0, j == TT - 1)
                        last.then_inc(pv_out, 1)

                    def m_scores(t):
                        tok = slice(t * P, (t + 1) * P)
                        pe.wait_ge(dbias, hd * (2 * TT) + (TT + t + 1))
                        if t == 0:
                            bank_split(6)
                            pe.wait_ge(rope_twice, lay + 1)
                            pe.wait_ge(rope_lo, h + (lay * (HEADS + 1) + 2))
                        product(ps[:, 2 + t, :], (qn_hi[:, tok], qn_lo[:, tok]), (kn_hi[:], kn_lo[:]), True, False)
                        pe.matmul(ps[:, 2 + t, :], qr[:, tok], kr_hi[:], start=False, stop=False)
                        pe.matmul(ps[:, 2 + t, :], qr[:, tok], kr_lo[:], start=False, stop=True)\
                            .then_inc(mscore, 1)

                    pe.wait_ge(mexp, hd * TT + BANKS)
                    def columns(s, bank):
                        split_unit(rnd, s)
                        for k in range(KB):
                            last = product(ps[:, bank, :], w(s, slice(k * P, (k + 1) * P)), xt(k),
                                           k == 0, k == KB - 1)
                        last.then_inc(used[s], 1)

                    columns(0, 2)
                    if more:
                        turn_rms(hd - 1)
                    else:
                        turn_latents()
                    columns(1, 3)
                    pe.wait_ge(latT_lo, lay * 3 + 3)
                    pe.wait_ge(rope_lo, h + (lay * (HEADS + 1) + 1))
                    pe.wait_ge(od_lo_done, hd + 1)
                    pe.wait_ge(om_lo_done, hd + 1)
                    split_unit(rnd, 3)
                    for k in range(2):
                        last = product(ps[:, 0, :], w(3, slice(k * MQ + MQ - P, (k + 1) * MQ)),
                                       (c_hi[:, k, :], c_lo[:, k, :]), k == 0, k == 1)
                    last.then_inc(proj_out, 1)
                    for k in range(2):
                        last = product(ps[:, 1, :], w(3, slice(k * MQ, k * MQ + NOPE)),
                                       (c_hi[:, k, :], c_lo[:, k, :]), k == 0, k == 1)
                    last.then_inc(proj_out, 1)
                    last = product(ps[:, 6, :], w(3, slice(2 * MQ, 2 * MQ + NOPE)),
                                   (c_hi[:, 2, :], c_lo[:, 2, :]), True, True)
                    last.then_inc(proj_out, 1)
                    bank_split(4)
                    d_scores(0)
                    d_scores(1)
                    columns(2, 7)
                    bank_split(6)
                    d_turn(0)
                    d_scores(2)
                    pe.wait_ge(rope_swapped, 2 * h + (lay * (2 * (HEADS + 1)) + 4))
                    pe.wait_ge(vt_copied, hd + 1)
                    for t in range(TT):
                        last = pe.transpose(ps[:, 0, t * P:(t + 1) * P], vt[:, t * P:(t + 1) * P], ident[:])
                    last.then_inc(vt_out, 1)
                    d_turn(1)
                    d_scores(3)
                    bank_split(5)
                    for t in range(TT):
                        tok = slice(t * P, (t + 1) * P)
                        last = product(ps[:, 1, tok], (c_hi[:, 2, tok], c_lo[:, 2, tok]),
                                       w(3, slice(2 * MQ + NOPE, 2 * MQ + NOPE + VD)), True, True)
                    last.then_inc(used[3], 1)
                    bank_split(7)
                    outs(0)
                    m_scores(0)
                    bank_split(8)
                    outs(1)
                    d_turn(2)
                    outs(2)
                    m_scores(1)
                    d_turn(3)
                    outs(3)
                    m_scores(2)
                    outs(4, 5)
                    m_scores(3)
                    outs(6, 7)
                    if more:
                        pe.wait_ge(wo_added, (hd - 1) * (2 * TT) + (BANKS + 7))
                    pv(0, 0, (vd_hi, vd_lo))
                    m_turn(0)
                    pv(1, 0, (vd_hi, vd_lo))
                    m_turn(1)
                    m_turn(2)
                    pe.wait_ge(sq_done, hd + 1)
                    pe.wait_ge(od_copied, hd + 1)
                    for t in range(TT):
                        last = pe.matmul(ps[:, 0, t:t + 1], sq[:, t * P:(t + 1) * P], ones[:], start=True,
                                         stop=True)
                    last.then_inc(ms_out, 1)
                    m_turn(3)
                    pe.wait_ge(mexp, hd * TT + (BANKS + 3))
                    pv(2, 4, (vm_hi, vm_lo))
                    pv(3, 4, (vm_hi, vm_lo))

                head(0, False)
                with pe.Fori(1, HEADS) as h:
                    head(h, True)
                rnd = pe.snap(lay * ROUNDS + (FR + HEADS))
                hd = pe.snap(lay * HEADS + (HEADS - 1))
                turn_rms(hd)
                for b in range(2 * TT):
                    out_sum(hd, rnd, b)
                turn_x(pe.snap(lay * LNS + 2), 0, (0, 1), wo_added, (lay + 1) * (HEADS * 2 * TT) + BANKS)
                ffn_pe(lay, 1, FR + 1 + HEADS)


_INS = ["x", "ffn1_w_gate", "ffn1_w_up", "ffn1_w_down", "ln1_g", "ln1_b", "w_in", "q_norm_g", "w_q_up",
        "kv_norm_g", "w_kv_up", "diff_lambda_q1", "diff_lambda_k1", "diff_lambda_q2", "diff_lambda_k2",
        "diff_subln_g", "w_out", "ln2_g", "ln2_b", "ffn2_w_gate", "ffn2_w_up", "ffn2_w_down", "ln3_g", "ln3_b"]


def constants():
    import math
    pos = np.arange(S, dtype=np.float32)
    inv = (np.float32(10000.0) ** (-np.arange(0, ROPE, 2, dtype=np.float32) / np.float32(ROPE))).astype(np.float32)
    ang = inv[:, None] * pos[None, :]
    c, s = np.cos(ang).astype(np.float32), np.sin(ang).astype(np.float32)
    part, col = np.arange(P)[:, None], np.arange(DIST)[None, :]
    init = [0.8 - 0.6 * math.exp(-0.3 * lay) for lay in range(DEPTH)]
    return {
        "ident": np.eye(P, dtype=np.float32),
        "alibi": (-np.abs(part - col + (S - P)) / DIFF_SCALE).astype(np.float32),
        "cos": np.concatenate([c, c]),
        "sin": np.concatenate([-s, s]),
        "lam": np.array([[v, 1.0 - v] for v in init], np.float32),
    }


def kernel(**inputs):
    import concourse.bacc as bacc
    from concourse.bass_utils import run_bass_kernel_spmd as run

    nc = bacc.Bacc("TRN2", target_bir_lowering=False, num_devices=1)
    arrays, args = {}, []
    for name in _INS:
        arrays[name] = np.ascontiguousarray(inputs[name])
    for name, a in constants().items():
        arrays["const_" + name] = a
    for name, a in arrays.items():
        args.append(nc.dram_tensor(name, a.shape, mybir.dt.from_np(a.dtype), kind="ExternalInput").ap())
    args.append(nc.dram_tensor("encoded", (1, S, D), F32, kind="ExternalOutput").ap())
    build(nc, *args)
    r = run(nc, [arrays], core_ids=[0])
    return r.results[0]["encoded"]
```
